# Optimizing a Trainium2 kernel written in Bass

```python
import jax
import jax.numpy as jnp
from jax import lax
import numpy as np
import jax, jax.numpy as jnp

D_MODEL = 1024
BATCH = 1
SEQ = 512
DEPTH = 1

EPS = 1e-6
ATTN_GROUPS = ((128, 1), (512, 4), (2048, 16))
N_GROUPS = 3
HEADS_PER_GROUP = 8
HEAD_DIM = 64
ATTN_WIDTH = HEADS_PER_GROUP * HEAD_DIM
N_ATTN_HEADS = N_GROUPS * HEADS_PER_GROUP
ATTN_QKV_COLS = N_GROUPS * 3 * ATTN_WIDTH
NUM_BUCKETS = 32
REL_MAX_DISTANCE = 1024
NEG_INF = -1e30
HG_HEADS = 8
HG_DK = D_MODEL // HG_HEADS
HG_DV = D_MODEL // HG_HEADS
HG_WIDTH = HG_HEADS * HG_DV
HG_CHUNK = 32
SPLIT_SIZES = (ATTN_QKV_COLS, ATTN_WIDTH, HG_WIDTH, HG_WIDTH, HG_WIDTH, HG_WIDTH, HG_WIDTH, D_MODEL, D_MODEL)
IN_COLS = ATTN_QKV_COLS + ATTN_WIDTH + 5 * HG_WIDTH + 2 * D_MODEL


def rms_norm(t, w):
    t32 = t.astype(jnp.float32)
    return t32 * lax.rsqrt(jnp.mean(t32 * t32, axis=-1, keepdims=True) + EPS) * w.astype(jnp.float32)

def t5_bucket(rel):
    half = NUM_BUCKETS // 2
    max_exact = half // 2
    n = np.abs(rel)
    large = max_exact + (np.log(np.maximum(n, 1) / max_exact)
                         / np.log(REL_MAX_DISTANCE / max_exact) * (half - max_exact)).astype(np.int32)
    large = np.minimum(large, half - 1)
    return np.where(rel > 0, half, 0) + np.where(n < max_exact, n, large)

def dilated_window_attention(q, k, v, bias_table, window, dilation):
    B, S, H, Dh = q.shape
    side = (window // 2) // dilation
    blk = side
    L = S // dilation
    nb = -(-L // blk)
    Lp = nb * blk

    def to_blocks(t):
        t = t.reshape(B, L, dilation, H, Dh)
        t = jnp.pad(t, ((0, 0), (0, Lp - L), (0, 0), (0, 0), (0, 0)))
        return t.reshape(B, nb, blk, dilation, H, Dh)

    def with_halo(t):
        tp = jnp.pad(t, ((0, 0), (1, 1), (0, 0), (0, 0), (0, 0), (0, 0)))
        return jnp.concatenate([tp[:, :-2], tp[:, 1:-1], tp[:, 2:]], axis=2)

    def from_blocks(t):
        t = t.reshape((B, Lp) + t.shape[3:])[:, :L]
        return t.reshape((B, S) + t.shape[3:])

    qb = to_blocks(q) * (HEAD_DIM ** -0.5)
    kh = with_halo(to_blocks(k))
    vh = with_halo(to_blocks(v))

    i_idx = np.arange(blk)[:, None]
    j_idx = np.arange(3 * blk)[None, :]
    rel = j_idx - blk - i_idx
    bias = jnp.transpose(bias_table[t5_bucket(rel * dilation)], (2, 0, 1))
    t_key = np.arange(nb)[:, None, None] * blk - blk + j_idx[None]
    valid = (np.abs(rel)[None] <= side) & (t_key >= 0) & (t_key < L)

    s = jnp.einsum('bnqrhd,bnkrhd->bnrhqk', qb, kh) + bias
    s = jnp.where(valid[None, :, None, None], s, NEG_INF)
    m = jnp.max(s, axis=-1, keepdims=True)
    p = jnp.exp(s - m)
    den = jnp.transpose(jnp.sum(p, axis=-1), (0, 1, 4, 2, 3))
    o = jnp.einsum('bnrhqk,bnkrhd->bnqrhd', p, vh) / den[..., None]
    m = jnp.transpose(m[..., 0], (0, 1, 4, 2, 3))
    return from_blocks(o), from_blocks(m), from_blocks(den)

def gla_chunk_scan(q, k, v, log_f):
    B, T, H, DK = q.shape
    DV = v.shape[-1]
    N = T // HG_CHUNK

    def chunks(t):
        return t.reshape(B, N, HG_CHUNK, H, t.shape[-1]).transpose(1, 0, 3, 2, 4)

    qc, kc, vc, gc = chunks(q), chunks(k), chunks(v), chunks(log_f)
    b = jnp.cumsum(gc, axis=3)
    b_last = b[:, :, :, -1, :]
    q_t = qc * jnp.exp(b)
    k_t = kc * jnp.exp(-b)
    k_s = kc * jnp.exp(b_last[:, :, :, None, :] - b)
    lower = jnp.tril(jnp.ones((HG_CHUNK, HG_CHUNK), dtype=bool))
    a = jnp.where(lower, jnp.einsum('nbhik,nbhjk->nbhij', q_t, k_t), 0.0)
    o_intra = jnp.einsum('nbhij,nbhjv->nbhiv', a, vc)

    def step(state, xs):
        q_n, k_n, v_n, dec_n = xs
        o_n = jnp.einsum('bhik,bhkv->bhiv', q_n, state)
        state = dec_n[..., None] * state + jnp.einsum('bhik,bhiv->bhkv', k_n, v_n)
        return state, o_n

    s0 = jnp.zeros((B, H, DK, DV), jnp.float32)
    _, o_inter = lax.scan(step, s0, (q_t, k_s, vc, jnp.exp(b_last)))
    o = o_intra + o_inter
    return o.transpose(1, 0, 3, 2, 4).reshape(B, T, H, DV)

def hgrn2_scan(q, i, z_f, lb):
    f = lb + (1.0 - lb) * jax.nn.sigmoid(z_f)
    return gla_chunk_scan(q, 1.0 - f, i, jnp.log(f))

def first_inputs(seed: int = 0) -> dict:
    key = jax.random.key(seed)
    ks = jax.random.split(key, 12)
    f32 = jnp.float32
    nrm = jax.random.normal
    return {
        "x": nrm(ks[0], (BATCH, SEQ, D_MODEL), f32),
        "norm_w": 1.0 + 0.02 * nrm(ks[1], (DEPTH, D_MODEL), f32),
        "w_in": nrm(ks[2], (DEPTH, D_MODEL, IN_COLS), f32) * D_MODEL ** -0.5,
        "q_norm_w": 1.0 + 0.02 * nrm(ks[3], (DEPTH, N_GROUPS, HEAD_DIM), f32),
        "k_norm_w": 1.0 + 0.02 * nrm(ks[4], (DEPTH, N_GROUPS, HEAD_DIM), f32),
        "rel_bias": 0.5 * nrm(ks[5], (NUM_BUCKETS, N_ATTN_HEADS), f32),
        "lb_fwd": 0.1 * nrm(ks[6], (DEPTH + 1, HG_HEADS * HG_DK), f32),
        "lb_bwd": 0.1 * nrm(ks[7], (DEPTH + 1, HG_HEADS * HG_DK), f32),
        "hg_norm_w": 1.0 + 0.02 * nrm(ks[8], (DEPTH, HG_DV), f32),
        "w_proj_a": nrm(ks[9], (DEPTH, ATTN_WIDTH, D_MODEL), f32) * ATTN_WIDTH ** -0.5,
        "w_proj_b": nrm(ks[10], (DEPTH, HG_WIDTH, D_MODEL), f32) * HG_WIDTH ** -0.5,
        "w_out": nrm(ks[11], (DEPTH, D_MODEL, D_MODEL), f32) * D_MODEL ** -0.5,
    }

def first_block(x, norm_w, w_in, q_norm_w, k_norm_w, rel_bias, lb_fwd, lb_bwd, hg_norm_w,
              w_proj_a, w_proj_b, w_out):
    f32 = jnp.float32
    B, S, _ = x.shape
    split_points = np.cumsum(SPLIT_SIZES)[:-1].tolist()
    lb_f_all = jnp.cumsum(jax.nn.softmax(lb_fwd.astype(f32), axis=0), axis=0)
    lb_b_all = jnp.cumsum(jax.nn.softmax(lb_bwd.astype(f32), axis=0), axis=0)
    bias_tab = rel_bias.astype(f32)
    h_res = x.astype(f32)
    for layer in range(DEPTH):
        h = rms_norm(h_res, norm_w[layer])
        z = jnp.einsum('bsd,dc->bsc', h, w_in[layer].astype(f32))
        qkv_a, g_a, q_b, zf_fwd, zf_bwd, i_b, g_b, zgate_a, zgate_b = jnp.split(z, split_points, axis=-1)

        qkv_a = qkv_a.reshape(B, S, N_GROUPS, 3, HEADS_PER_GROUP, HEAD_DIM)
        outs, maxes, dens = [], [], []
        for g, (window, dilation) in enumerate(ATTN_GROUPS):
            q = rms_norm(qkv_a[:, :, g, 0], q_norm_w[layer, g])
            k = rms_norm(qkv_a[:, :, g, 1], k_norm_w[layer, g])
            v = qkv_a[:, :, g, 2]
            o_g, m_g, d_g = dilated_window_attention(
                q, k, v, bias_tab[:, g * HEADS_PER_GROUP:(g + 1) * HEADS_PER_GROUP], window, dilation)
            outs.append(o_g)
            maxes.append(m_g)
            dens.append(d_g)
        m_all = jnp.stack(maxes)
        wts = jnp.stack(dens) * jnp.exp(m_all - jnp.max(m_all, axis=0, keepdims=True))
        o_a = jnp.sum(wts[..., None] * jnp.stack(outs), axis=0) / jnp.sum(wts, axis=0)[..., None]
        y_a = jnp.einsum('bsc,cd->bsd', o_a.reshape(B, S, ATTN_WIDTH) * jax.nn.silu(g_a),
                         w_proj_a[layer].astype(f32))

        q_b = q_b.reshape(B, S, HG_HEADS, HG_DK)
        i_b = i_b.reshape(B, S, HG_HEADS, HG_DV)
        zf_fwd = zf_fwd.reshape(B, S, HG_HEADS, HG_DK)
        zf_bwd = zf_bwd.reshape(B, S, HG_HEADS, HG_DK)
        lb_f = lb_f_all[layer].reshape(HG_HEADS, HG_DK)
        lb_b = lb_b_all[layer].reshape(HG_HEADS, HG_DK)
        o_fwd = hgrn2_scan(q_b, i_b, zf_fwd, lb_f)
        o_bwd = jnp.flip(hgrn2_scan(jnp.flip(q_b, 1), jnp.flip(i_b, 1), jnp.flip(zf_bwd, 1), lb_b), 1)
        o_b = rms_norm(o_fwd + o_bwd, hg_norm_w[layer]) * jax.nn.silu(g_b.reshape(B, S, HG_HEADS, HG_DV))
        y_b = jnp.einsum('bsc,cd->bsd', o_b.reshape(B, S, HG_WIDTH), w_proj_b[layer].astype(f32))

        merged = jax.nn.sigmoid(zgate_a) * y_a + jax.nn.sigmoid(zgate_b) * y_b
        h_res = h_res + jnp.einsum('bsd,de->bse', merged, w_out[layer].astype(f32))
    return h_res.astype(x.dtype)


DEPTH_2 = 2

GRID_W = 64
CTX_LEN = 256
ROPE_BASE = 10000.0
Q_BLOCK = 128

MLA_HEADS = D_MODEL // 128
MLA_NOPE = 64
MLA_ROPE = 32
MLA_QK = MLA_NOPE + MLA_ROPE
MLA_V = 64
Q_LORA = 3 * D_MODEL // 8
KV_LORA = D_MODEL // 4
MLA_IN = Q_LORA + KV_LORA + MLA_ROPE
CONV_CH = D_MODEL // 2
CONV_K = 31
EVEN_IN = MLA_IN + 2 * CONV_CH
EVEN_OUT = MLA_HEADS * MLA_V + CONV_CH

RW_N = 64
RW_HEADS = D_MODEL // 128
RW_DIM = RW_HEADS * RW_N
DECAY_LORA = 64
ICLR_LORA = 64
GATE_LORA = 128
SHIFT_K = 3
RW_IN = 3 * RW_DIM + 2 * DECAY_LORA + 2 * ICLR_LORA + GATE_LORA
GN_EPS = 64e-5

NA_HEADS = D_MODEL // 128
NA_DIM = 64
WIN_H = 8
WIN_W = 16
NA_IN = 3 * NA_HEADS * NA_DIM
ODD_IN = RW_IN + NA_IN
ODD_OUT = RW_DIM + NA_HEADS * NA_DIM

N_EXPERTS = 16
D_EXPERT = D_MODEL
EC_FACTOR = 2


def rms_norm_2(x, g):
    xf = x.astype(jnp.float32)
    y = xf * lax.rsqrt(jnp.mean(jnp.square(xf), -1, keepdims=True) + EPS)
    return (y * g.astype(jnp.float32)).astype(x.dtype)

def layer_norm(x, g, b):
    xf = x.astype(jnp.float32)
    mu = jnp.mean(xf, -1, keepdims=True)
    var = jnp.mean(jnp.square(xf - mu), -1, keepdims=True)
    y = (xf - mu) * lax.rsqrt(var + EPS)
    return (y * g.astype(jnp.float32) + b.astype(jnp.float32)).astype(x.dtype)

def head_group_norm(y, g, b):
    B, T, H, N = y.shape
    mu = jnp.mean(y, -1, keepdims=True)
    var = jnp.mean(jnp.square(y - mu), -1, keepdims=True)
    yn = ((y - mu) * lax.rsqrt(var + GN_EPS)).reshape(B, T, H * N)
    return yn * g + b

def depthwise_conv(x, w):
    pad = (w.shape[0] - 1) // 2
    return lax.conv_general_dilated(x, w[:, None, :].astype(x.dtype), (1,), [(pad, pad)],
                                    dimension_numbers=('NWC', 'WIO', 'NWC'),
                                    feature_group_count=x.shape[-1])

def axial_rope_tables(n_tok, rot_dim):
    t = jnp.arange(n_tok, dtype=jnp.int32)
    row = (t // GRID_W).astype(jnp.float32)
    col = (t % GRID_W).astype(jnp.float32)
    half = rot_dim // 2
    inv = ROPE_BASE ** (-jnp.arange(0, half, 2, dtype=jnp.float32) / half)
    ar = row[:, None] * inv
    ac = col[:, None] * inv
    ang = jnp.concatenate([ar, ar, ac, ac], -1)
    return jnp.cos(ang), jnp.sin(ang)

def rotate_half(u):
    u1, u2 = jnp.split(u, 2, -1)
    return jnp.concatenate([-u2, u1], -1)

def apply_axial_rope(x, cos, sin):
    half = x.shape[-1] // 2
    rot = jnp.concatenate([rotate_half(x[..., :half]), rotate_half(x[..., half:])], -1)
    return (x * cos[:, None, :] + rot * sin[:, None, :]).astype(x.dtype)

def dense_attention(q, k, v):
    scale = q.shape[-1] ** -0.5
    s = jnp.einsum('bqhd,bkhd->bhqk', q, k).astype(jnp.float32) * scale
    p = jax.nn.softmax(s, -1).astype(v.dtype)
    return jnp.einsum('bhqk,bkhd->bqhd', p, v)

def blocked_attention(q, k, v):
    B, T, H, D = q.shape
    nb = T // Q_BLOCK
    qb = jnp.moveaxis(q.reshape(B, nb, Q_BLOCK, H, D), 1, 0)
    out = lax.map(lambda qq: dense_attention(qq, k, v), qb)
    return jnp.moveaxis(out, 0, 1).reshape(B, T, H, v.shape[-1])

def mla_qkv(u, q_norm, w_uq, kv_norm, w_ukv, q_g, k_g, rope_cs=None):
    B, T, _ = u.shape
    cq = u[..., :Q_LORA]
    ckv = u[..., Q_LORA:Q_LORA + KV_LORA]
    kr = u[..., Q_LORA + KV_LORA:MLA_IN]
    q = (rms_norm_2(cq, q_norm) @ w_uq).reshape(B, T, MLA_HEADS, MLA_QK)
    kv = (rms_norm_2(ckv, kv_norm) @ w_ukv).reshape(B, T, MLA_HEADS, MLA_NOPE + MLA_V)
    k_nope, v = kv[..., :MLA_NOPE], kv[..., MLA_NOPE:]
    k = jnp.concatenate([k_nope, jnp.broadcast_to(kr[:, :, None, :], (B, T, MLA_HEADS, MLA_ROPE))], -1)
    q = rms_norm_2(q, q_g)
    k = rms_norm_2(k, k_g)
    if rope_cs is not None:
        cos, sin = rope_cs
        q = jnp.concatenate([q[..., :MLA_NOPE], apply_axial_rope(q[..., MLA_NOPE:], cos, sin)], -1)
        k = jnp.concatenate([k[..., :MLA_NOPE], apply_axial_rope(k[..., MLA_NOPE:], cos, sin)], -1)
    return q, k, v

def conformer_conv(u, dw_w, dw_b, ln_g, ln_b):
    a, gate = jnp.split(u, 2, -1)
    h = a * jax.nn.sigmoid(gate)
    h = depthwise_conv(h, dw_w) + dw_b
    return jax.nn.silu(layer_norm(h, ln_g, ln_b))

def even_mixer(h, hc, rope_cs, w_in, w_out, q_norm, w_uq, kv_norm, w_ukv, q_g, k_g,
               dw_w, dw_b, ln_g, ln_b, with_ctx_out):
    B, T, _ = h.shape
    u = h @ w_in
    uc = hc @ w_in
    mla_p = (q_norm, w_uq, kv_norm, w_ukv, q_g, k_g)
    q, k, v = mla_qkv(u[..., :MLA_IN], *mla_p, rope_cs=rope_cs)
    qc, kc, vc = mla_qkv(uc[..., :MLA_IN], *mla_p)
    o_att = blocked_attention(q, jnp.concatenate([k, kc], 1), jnp.concatenate([v, vc], 1))
    o_conv = conformer_conv(u[..., MLA_IN:], dw_w, dw_b, ln_g, ln_b)
    y = jnp.concatenate([o_att.reshape(B, T, -1), o_conv], -1) @ w_out
    if not with_ctx_out:
        return y, None
    oc_att = dense_attention(qc, kc, vc)
    oc_conv = conformer_conv(uc[..., MLA_IN:], dw_w, dw_b, ln_g, ln_b)
    yc = jnp.concatenate([oc_att.reshape(B, hc.shape[1], -1), oc_conv], -1) @ w_out
    return y, yc

def wkv7_step(S, inp):
    r, w, k, v, a, b = inp
    sa = jnp.einsum('bhvk,bhk->bhv', S, a)
    S = S * w[:, :, None, :] + sa[..., None] * b[:, :, None, :] + v[..., None] * k[:, :, None, :]
    return S, jnp.einsum('bhvk,bhk->bhv', S, r)

def wkv7_scan(S0, r, w, k, v, a, b, reverse):
    xs = tuple(jnp.moveaxis(t.astype(jnp.float32), 1, 0) for t in (r, w, k, v, a, b))
    S, ys = lax.scan(wkv7_step, S0, xs, reverse=reverse)
    return S, jnp.moveaxis(ys, 0, 1)

def rwkv_inputs(u, shift_w, w0, w2, a0, a2, g2, k_k, k_a):
    u = depthwise_conv(u, shift_w)
    B, T, _ = u.shape
    o1 = 3 * RW_DIM
    o2 = o1 + 2 * DECAY_LORA
    o3 = o2 + 2 * ICLR_LORA
    r, k, v = jnp.split(u[..., :o1], 3, axis=-1)
    lw = u[..., o1:o2].reshape(B, T, 2, DECAY_LORA)
    la = u[..., o2:o3].reshape(B, T, 2, ICLR_LORA)
    lg = u[..., o3:]
    logw = (w0 + jnp.einsum('btdr,drc->btdc', jnp.tanh(lw), w2)).astype(jnp.float32)
    w = jnp.exp(-jnp.exp(-jax.nn.softplus(-logw) - 0.5))
    a = jax.nn.sigmoid((a0 + jnp.einsum('btdr,drc->btdc', la, a2)).astype(jnp.float32))
    kk = (k * k_k).reshape(B, T, RW_HEADS, RW_N).astype(jnp.float32)
    kk = kk * lax.rsqrt(jnp.sum(kk * kk, -1, keepdims=True) + 1e-12)
    k_eff = k[:, :, None, :].astype(jnp.float32) * (1.0 + (a - 1.0) * k_a)
    g = jax.nn.sigmoid(lg) @ g2
    hd = lambda t: t.reshape(B, T, RW_HEADS, RW_N).astype(jnp.float32)
    dir_hd = lambda t: t.reshape(B, T, 2, RW_HEADS, RW_N)
    return hd(r), hd(v), kk, dir_hd(w), dir_hd(a), dir_hd(k_eff), g

def rwkv_mixer(u, uc, shift_w, w0, w2, a0, a2, g2, k_k, k_a, r_k, gn_g, gn_b, with_ctx_out):
    p = (shift_w, w0, w2, a0, a2, g2, k_k, k_a)
    lat = rwkv_inputs(u, *p)
    cx = rwkv_inputs(uc, *p)
    rk = r_k.reshape(RW_HEADS, RW_N).astype(jnp.float32)
    B = u.shape[0]

    def direction(inp, d, S0):
        r, v, kk, w, a, k_eff, _ = inp
        a_d, k_d = a[:, :, d], k_eff[:, :, d]
        S, y = wkv7_scan(S0, r, w[:, :, d], k_d, v, -kk, kk * a_d, reverse=(d == 1))
        return S, y + jnp.sum(r * k_d * rk, -1, keepdims=True) * v

    y_lat, y_ctx = [], []
    for d in range(2):
        S0 = jnp.zeros((B, RW_HEADS, RW_N, RW_N), jnp.float32)
        S_c, yc_d = direction(cx, d, S0)
        _, yl_d = direction(lat, d, S_c)
        y_lat.append(yl_d)
        y_ctx.append(yc_d)
    y = head_group_norm(y_lat[0] + y_lat[1], gn_g, gn_b) * lat[6]
    if not with_ctx_out:
        return y, None
    yc = head_group_norm(y_ctx[0] + y_ctx[1], gn_g, gn_b) * cx[6]
    return y, yc

def natten_qkv(u, q_g, k_g):
    B, T, _ = u.shape
    q, k, v = [t.reshape(B, T, NA_HEADS, NA_DIM) for t in jnp.split(u, 3, -1)]
    return rms_norm_2(q, q_g), rms_norm_2(k, k_g), v

def neighbourhood_attention(q, k, v, k_ctx, v_ctx, rpb):
    B, T, H, Dh = q.shape
    rows = T // GRID_W
    kh = min(WIN_H, rows)
    kw = min(WIN_W, GRID_W)
    n_loc = kh * kw
    scale = Dh ** -0.5
    qg = q.reshape(B, rows, GRID_W, H, Dh)
    kg = k.reshape(B, rows, GRID_W, H, Dh)
    vg = v.reshape(B, rows, GRID_W, H, Dh)
    cols = jnp.arange(GRID_W, dtype=jnp.int32)
    col_start = jnp.clip(cols - kw // 2, 0, GRID_W - kw)
    col_idx = col_start[:, None] + jnp.arange(kw, dtype=jnp.int32)[None, :]
    dcol = col_idx - cols[:, None] + (WIN_W - 1)

    def one_row(r):
        rs = jnp.clip(r - kh // 2, 0, rows - kh)
        k_band = lax.dynamic_slice_in_dim(kg, rs, kh, axis=1)
        v_band = lax.dynamic_slice_in_dim(vg, rs, kh, axis=1)
        k_win = k_band[:, :, col_idx]
        v_win = v_band[:, :, col_idx]
        q_row = lax.dynamic_index_in_dim(qg, r, axis=1, keepdims=False)
        drow = rs + jnp.arange(kh, dtype=jnp.int32) - r + (WIN_H - 1)
        bias = jnp.transpose(rpb[:, drow][:, :, dcol], (0, 2, 1, 3))
        s_loc = jnp.einsum('bchd,bicjhd->bhcij', q_row, k_win).astype(jnp.float32) * scale + bias.astype(jnp.float32)
        s_ctx = jnp.einsum('bchd,bnhd->bhcn', q_row, k_ctx).astype(jnp.float32) * scale
        s = jnp.concatenate([s_loc.reshape(B, H, GRID_W, n_loc), s_ctx], -1)
        p = jax.nn.softmax(s, -1).astype(v.dtype)
        o = jnp.einsum('bhcij,bicjhd->bchd', p[..., :n_loc].reshape(B, H, GRID_W, kh, kw), v_win)
        return o + jnp.einsum('bhcn,bnhd->bchd', p[..., n_loc:], v_ctx)

    out = lax.map(one_row, jnp.arange(rows, dtype=jnp.int32))
    return jnp.moveaxis(out, 0, 1).reshape(B, T, H, Dh)

def odd_mixer(h, hc, w_in, w_out, shift_w, w0, w2, a0, a2, g2, k_k, k_a, r_k, gn_g, gn_b,
              q_g, k_g, rpb, with_ctx_out):
    B, T, _ = h.shape
    u = h @ w_in
    uc = hc @ w_in
    y_rw, yc_rw = rwkv_mixer(u[..., :RW_IN], uc[..., :RW_IN], shift_w, w0, w2, a0, a2, g2,
                             k_k, k_a, r_k, gn_g, gn_b, with_ctx_out)
    q, k, v = natten_qkv(u[..., RW_IN:], q_g, k_g)
    qc, kc, vc = natten_qkv(uc[..., RW_IN:], q_g, k_g)
    y_na = neighbourhood_attention(q, k, v, kc, vc, rpb)
    y = jnp.concatenate([y_rw, y_na.reshape(B, T, -1)], -1) @ w_out
    if not with_ctx_out:
        return y, None
    yc_na = dense_attention(qc, kc, vc)
    yc = jnp.concatenate([yc_rw, yc_na.reshape(B, hc.shape[1], -1)], -1) @ w_out
    return y, yc

def expert_choice_ffn(h, router, w1, w3, w2):
    B, T, D = h.shape
    cap = max(1, EC_FACTOR * T // N_EXPERTS)
    aff = jax.nn.softmax(jnp.einsum('btd,de->bte', h, router).astype(jnp.float32), -1)
    gate, idx = lax.top_k(jnp.swapaxes(aff, 1, 2), cap)
    xs = jax.vmap(lambda hb, ib: hb[ib])(h, idx)
    hid = jax.nn.silu(jnp.einsum('becd,edf->becf', xs, w1)) * jnp.einsum('becd,edf->becf', xs, w3)
    ys = jnp.einsum('becf,efd->becd', hid, w2) * gate[..., None].astype(h.dtype)
    return jax.vmap(lambda yb, ib: jnp.zeros((T, D), yb.dtype).at[ib.reshape(-1)].add(yb.reshape(-1, D)))(ys, idx)

def second_inputs(seed: int = 0) -> dict:
    key = jax.random.key(seed)
    keys = iter(jax.random.split(key, 64))

    def nrm(shape, scale):
        return jax.random.normal(next(keys), shape, jnp.float32) * scale

    def gain(shape):
        return 1.0 + nrm(shape, 0.05)

    ne, no = (DEPTH_2 + 1) // 2, DEPTH_2 // 2
    d = D_MODEL
    shift_base = jnp.array([0.25, 0.5, 0.25], jnp.float32)[None, :, None]
    return {
        'x': nrm((BATCH, SEQ, d), 1.0),
        'c': nrm((BATCH, d), 1.0),
        'ctx': nrm((BATCH, CTX_LEN, d), 1.0),
        'c_ctx': nrm((d,), 1.0),
        'ada_w': nrm((DEPTH_2, d, 6 * d), 0.5 * d ** -0.5),
        'ada_b': nrm((DEPTH_2, 6 * d), 0.02),
        'norm1_g': gain((DEPTH_2, d)),
        'norm2_g': gain((DEPTH_2, d)),
        'ev_w_in': nrm((ne, d, EVEN_IN), d ** -0.5),
        'ev_w_out': nrm((ne, EVEN_OUT, d), EVEN_OUT ** -0.5),
        'mla_q_norm': gain((ne, Q_LORA)),
        'mla_w_uq': nrm((ne, Q_LORA, MLA_HEADS * MLA_QK), Q_LORA ** -0.5),
        'mla_kv_norm': gain((ne, KV_LORA)),
        'mla_w_ukv': nrm((ne, KV_LORA, MLA_HEADS * (MLA_NOPE + MLA_V)), KV_LORA ** -0.5),
        'mla_q_g': gain((ne, MLA_QK)),
        'mla_k_g': gain((ne, MLA_QK)),
        'cv_dw_w': nrm((ne, CONV_K, CONV_CH), CONV_K ** -0.5),
        'cv_dw_b': nrm((ne, CONV_CH), 0.02),
        'cv_ln_g': gain((ne, CONV_CH)),
        'cv_ln_b': nrm((ne, CONV_CH), 0.02),
        'od_w_in': nrm((no, d, ODD_IN), d ** -0.5),
        'od_w_out': nrm((no, ODD_OUT, d), ODD_OUT ** -0.5),
        'rw_shift_w': shift_base + nrm((no, SHIFT_K, RW_IN), 0.1),
        'rw_w0': jax.random.uniform(next(keys), (no, 2, RW_DIM), jnp.float32, -4.0, 1.0),
        'rw_w2': nrm((no, 2, DECAY_LORA, RW_DIM), 0.5 * DECAY_LORA ** -0.5),
        'rw_a0': nrm((no, 2, RW_DIM), 0.5),
        'rw_a2': nrm((no, 2, ICLR_LORA, RW_DIM), 0.5 * ICLR_LORA ** -0.5),
        'rw_g2': nrm((no, GATE_LORA, RW_DIM), GATE_LORA ** -0.5),
        'rw_k_k': 0.85 + nrm((no, RW_DIM), 0.05),
        'rw_k_a': gain((no, RW_DIM)),
        'rw_r_k': nrm((no, RW_DIM), 0.3),
        'rw_gn_g': gain((no, RW_DIM)),
        'rw_gn_b': nrm((no, RW_DIM), 0.02),
        'na_q_g': gain((no, NA_DIM)),
        'na_k_g': gain((no, NA_DIM)),
        'na_rpb': nrm((no, NA_HEADS, 2 * WIN_H - 1, 2 * WIN_W - 1), 0.5),
        'moe_router': nrm((DEPTH_2, d, N_EXPERTS), d ** -0.5),
        'moe_w1': nrm((DEPTH_2, N_EXPERTS, d, D_EXPERT), d ** -0.5),
        'moe_w3': nrm((DEPTH_2, N_EXPERTS, d, D_EXPERT), d ** -0.5),
        'moe_w2': nrm((DEPTH_2, N_EXPERTS, D_EXPERT, d), D_EXPERT ** -0.5),
    }

def second_block(x, c, ctx, c_ctx, ada_w, ada_b, norm1_g, norm2_g,
              ev_w_in, ev_w_out, mla_q_norm, mla_w_uq, mla_kv_norm, mla_w_ukv, mla_q_g, mla_k_g,
              cv_dw_w, cv_dw_b, cv_ln_g, cv_ln_b,
              od_w_in, od_w_out, rw_shift_w, rw_w0, rw_w2, rw_a0, rw_a2, rw_g2, rw_k_k, rw_k_a, rw_r_k,
              rw_gn_g, rw_gn_b, na_q_g, na_k_g, na_rpb,
              moe_router, moe_w1, moe_w3, moe_w2):
    rope_cs = axial_rope_tables(x.shape[1], MLA_ROPE)
    for i in range(DEPTH_2):
        last = i == DEPTH_2 - 1
        j = i // 2
        mod = jnp.einsum('bd,de->be', jax.nn.silu(c), ada_w[i]) + ada_b[i]
        mod_c = jax.nn.silu(c_ctx) @ ada_w[i] + ada_b[i]
        sh1, sc1, g1, sh2, sc2, g2 = jnp.split(mod[:, None, :], 6, -1)
        csh1, csc1, cg1, csh2, csc2, cg2 = jnp.split(mod_c[None, None, :], 6, -1)
        h = rms_norm_2(x, norm1_g[i]) * (1.0 + sc1) + sh1
        hc = rms_norm_2(ctx, norm1_g[i]) * (1.0 + csc1) + csh1
        if i % 2 == 0:
            y, yc = even_mixer(h, hc, rope_cs, ev_w_in[j], ev_w_out[j], mla_q_norm[j], mla_w_uq[j],
                               mla_kv_norm[j], mla_w_ukv[j], mla_q_g[j], mla_k_g[j],
                               cv_dw_w[j], cv_dw_b[j], cv_ln_g[j], cv_ln_b[j], not last)
        else:
            y, yc = odd_mixer(h, hc, od_w_in[j], od_w_out[j], rw_shift_w[j], rw_w0[j], rw_w2[j],
                              rw_a0[j], rw_a2[j], rw_g2[j], rw_k_k[j], rw_k_a[j], rw_r_k[j],
                              rw_gn_g[j], rw_gn_b[j], na_q_g[j], na_k_g[j], na_rpb[j], not last)
        x = x + g1 * y
        h = rms_norm_2(x, norm2_g[i]) * (1.0 + sc2) + sh2
        x = x + g2 * expert_choice_ffn(h, moe_router[i], moe_w1[i], moe_w3[i], moe_w2[i])
        if not last:
            ctx = ctx + cg1 * yc
            hc = rms_norm_2(ctx, norm2_g[i]) * (1.0 + csc2) + csh2
            ctx = ctx + cg2 * expert_choice_ffn(hc, moe_router[i], moe_w1[i], moe_w3[i], moe_w2[i])
    return x


def setup_inputs(seed=0):
    out = dict(first_inputs(seed))
    for name, value in second_inputs(seed + 1).items():
        if name != "x":
            out[name + "_2"] = value
    return out


def reference(
    x, norm_w, w_in, q_norm_w, k_norm_w, rel_bias, lb_fwd, lb_bwd, hg_norm_w, w_proj_a,
    w_proj_b, w_out, c_2, ctx_2, c_ctx_2, ada_w_2, ada_b_2, norm1_g_2, norm2_g_2, ev_w_in_2,
    ev_w_out_2, mla_q_norm_2, mla_w_uq_2, mla_kv_norm_2, mla_w_ukv_2, mla_q_g_2, mla_k_g_2,
    cv_dw_w_2, cv_dw_b_2, cv_ln_g_2, cv_ln_b_2, od_w_in_2, od_w_out_2, rw_shift_w_2, rw_w0_2,
    rw_w2_2, rw_a0_2, rw_a2_2, rw_g2_2, rw_k_k_2, rw_k_a_2, rw_r_k_2, rw_gn_g_2, rw_gn_b_2,
    na_q_g_2, na_k_g_2, na_rpb_2, moe_router_2, moe_w1_2, moe_w3_2, moe_w2_2,
):
    x = first_block(
        x, norm_w, w_in, q_norm_w, k_norm_w, rel_bias, lb_fwd, lb_bwd, hg_norm_w, w_proj_a,
        w_proj_b, w_out,
    )
    return second_block(
        x, c_2, ctx_2, c_ctx_2, ada_w_2, ada_b_2, norm1_g_2, norm2_g_2, ev_w_in_2, ev_w_out_2,
        mla_q_norm_2, mla_w_uq_2, mla_kv_norm_2, mla_w_ukv_2, mla_q_g_2, mla_k_g_2, cv_dw_w_2,
        cv_dw_b_2, cv_ln_g_2, cv_ln_b_2, od_w_in_2, od_w_out_2, rw_shift_w_2, rw_w0_2, rw_w2_2,
        rw_a0_2, rw_a2_2, rw_g2_2, rw_k_k_2, rw_k_a_2, rw_r_k_2, rw_gn_g_2, rw_gn_b_2, na_q_g_2,
        na_k_g_2, na_rpb_2, moe_router_2, moe_w1_2, moe_w3_2, moe_w2_2,
    )


_drawn_inputs = setup_inputs


def setup_inputs(seed=0):
    import zlib

    import numpy as np

    out = dict(_drawn_inputs(seed))
    spreads = {}
    factors = {'norm_w': 3.387,
     'q_norm_w': 8.0,
     'k_norm_w': 8.0,
     'rel_bias': 3.243,
     'lb_fwd': 2.718,
     'lb_bwd': 2.696,
     'hg_norm_w': 6.39,
     'ada_b_2': 3.071,
     'norm1_g_2': 4.514,
     'norm2_g_2': 3.748,
     'mla_q_norm_2': 8.0,
     'mla_w_uq_2': 3.321,
     'mla_kv_norm_2': 8.0,
     'mla_q_g_2': 8.0,
     'mla_k_g_2': 8.0,
     'cv_dw_b_2': 8.0,
     'cv_ln_g_2': 6.342,
     'cv_ln_b_2': 27.902,
     'rw_w2_2': 7.208,
     'rw_a2_2': 3.444,
     'rw_k_k_2': 200.0,
     'rw_k_a_2': 30.043,
     'rw_r_k_2': 3.926,
     'rw_gn_g_2': 64.0,
     'rw_gn_b_2': 200.0,
     'na_q_g_2': 21.482,
     'na_k_g_2': 22.069,
     'na_rpb_2': 25.338,
     'rw_a0_2': 3.941}
    for name, (base, spread) in spreads.items():
        noise = np.random.default_rng([zlib.crc32(name.encode()), seed]).standard_normal(out[name].shape)
        drawn = base * np.exp(spread * noise) if base else spread * noise
        out[name] = jnp.asarray(drawn.astype(out[name].dtype))
    for name, factor in factors.items():
        out[name] = (out[name] * factor).astype(out[name].dtype)
    return out
```

```python
from contextlib import ExitStack, contextmanager

import numpy as np
import concourse.bass as bass
from concourse import mybir

F32 = mybir.dt.float32
I32 = mybir.dt.int32
U32 = mybir.dt.uint32
ALU = mybir.AluOpType
ACT = mybir.ActivationFunctionType
AX = mybir.AxisListType

P = 128
D = 1024
KT = D // P
SEQ = 512
CTX = 256
NT = SEQ // P
NC = CTX // P
NX = NT + NC
ALLTOK = SEQ + CTX
EPS = 1e-6
GN_EPS = 64e-5
NEG = -1e30
BANKS = 6
BANK = 512

GROUPS = ((128, 1), (512, 4), (2048, 16))
NG = len(GROUPS)
AH = 8
HD = 64
AW = AH * HD
BUCKETS = 32
REL_MAX = 1024
HH = 8
HDK = D // HH
GLA_CHUNK = 32
OFF_GA = NG * 3 * AW
OFF_Q = OFF_GA + AW
OFF_ZF = OFF_Q + D
OFF_ZB = OFF_ZF + D
OFF_I = OFF_ZB + D
OFF_GB = OFF_I + D
OFF_ZGA = OFF_GB + D
OFF_ZGB = OFF_ZGA + D

MH, NOPE, ROPE, MV = 8, 64, 32, 64
MQK = NOPE + ROPE
QL, KVL = 3 * D // 8, D // 4
MLA_IN = QL + KVL + ROPE
CONV_CH, CONV_K = D // 2, 31
GRID_W = 64

RH, RN = 8, 64
RD = RH * RN
LORA = 64
RW_IN = 3 * RD + 4 * LORA + 128
NA_H, NA_D, WIN_H, WIN_W = 8, 64, 8, 16

NE = 16
CAP_X = 2 * SEQ // NE
CAP_C = 2 * CTX // NE



class Signal:

    def __init__(self, nc, name):
        self.sem = nc.alloc_semaphore(name)
        self.n = 0

    def one(self):
        self.n += 1
        return 1

    def sixteen(self):
        self.n += 16
        return 16


class Core:
    def __init__(self, nc):
        self.nc = nc
        self.step = Signal(nc, "step_done")
        self.landed = Signal(nc, "data_landed")
        self.stored = Signal(nc, "data_stored")
        self.filled = Signal(nc, "bank_filled")
        self.emptied_v = Signal(nc, "bank_emptied_by_vector")
        self.emptied_s = Signal(nc, "bank_emptied_by_scalar")
        self.link_v = Signal(nc, "vector_link")
        self.link_s = Signal(nc, "scalar_link")
        self.weights = [Signal(nc, f"weights_landed_{i}") for i in range(3)]
        self.bank = [nc.alloc_psum_tensor(f"bank{i}", [P, BANK], F32) for i in range(8)]
        self.names = 0

    def load(self, dst, src):
        sp = self.nc.sync
        sp.wait_ge(self.step.sem, self.step.n)
        sp.wait_ge(self.stored.sem, self.stored.n)
        sp.dma_start(dst, src, allow_slow_non_contiguous=True).then_inc(self.landed.sem, self.landed.sixteen())

    def store(self, dst, src):
        sp = self.nc.sync
        sp.wait_ge(self.step.sem, self.step.n)
        sp.wait_ge(self.landed.sem, self.landed.n)
        sp.wait_ge(self.stored.sem, self.stored.n)
        sp.dma_start(dst, src, allow_slow_non_contiguous=True).then_inc(self.stored.sem, self.stored.sixteen())

    @contextmanager
    def scope(self):
        with ExitStack() as es:
            def sb(name, shape, dt=F32):
                self.names += 1
                return es.enter_context(self.nc.sbuf_tensor(f"{name}_{self.names}", list(shape), dt))
            yield sb


def linked(eng, sig, ins):
    ins.then_inc(sig.sem, sig.one())
    eng.wait_ge(sig.sem, sig.n)


def bc(ap, n):
    return bass.AP(ap.tensor, ap.offset, [list(x) for x in ap.ap] + [[0, n]])


def mid(ap, n):
    a = [list(x) for x in ap.ap]
    return bass.AP(ap.tensor, ap.offset, [a[0], [0, n]] + a[1:])


def dram(ap, offset, pattern):
    return bass.AP(ap.tensor, ap.offset + offset, [list(x) for x in pattern])


def load_rows(core, dst, src, offset, n):
    core.load(dst, dram(src, offset, [[0, P], [1, n]]))


def load_columns(core, dst, src, offset, tiles):
    core.load(dst, dram(src, offset, [[1, P], [P, tiles]]))


def products(core, n, fill, take, who=None, chunks=0, load=None, last_of=None, first_of=None, ring=2):
    who = who or (lambda i: "v")
    v_before = [sum(who(j) == "v" for j in range(i)) for i in range(n + 1)]
    f0, v0, s0 = core.filled.n, core.emptied_v.n, core.emptied_s.n
    w0 = [w.n for w in core.weights]
    nc = core.nc
    with nc.Block() as block:
        if chunks:
            @block.sync
            def _(sp):
                sp.wait_ge(core.step.sem, core.step.n)
                sp.wait_ge(core.landed.sem, core.landed.n)
                sp.wait_ge(core.stored.sem, core.stored.n)
                for c in range(chunks):
                    if c >= ring:
                        sp.wait_ge(core.filled.sem, f0 + last_of(c - ring) + 1)
                    for ins in load(sp, c):
                        ins.then_inc(core.weights[c % ring].sem, core.weights[c % ring].sixteen())

        ready = {}
        if chunks:
            total = list(w0)
            per = [core.weights[r].n for r in range(ring)]
            counts = [0] * ring
            for c in range(chunks):
                counts[c % ring] += 1
            share = [(per[r] - w0[r]) // max(counts[r], 1) for r in range(ring)]
            for c in range(chunks):
                total[c % ring] += share[c % ring]
                ready[first_of(c)] = (core.weights[c % ring], total[c % ring])

        @block.tensor
        def _(pe):
            pe.wait_ge(core.step.sem, core.step.n)
            pe.wait_ge(core.landed.sem, core.landed.n)
            pe.wait_ge(core.stored.sem, core.stored.n)
            for i in range(n):
                if i in ready:
                    pe.wait_ge(ready[i][0].sem, ready[i][1])
                if i >= BANKS:
                    j = i - BANKS
                    if who(j) == "v":
                        pe.wait_ge(core.emptied_v.sem, v0 + v_before[j] + 1)
                    else:
                        pe.wait_ge(core.emptied_s.sem, s0 + j - v_before[j] + 1)
                fill(pe, i, core.bank[i % BANKS]).then_inc(core.filled.sem, core.filled.one())

        @block.vector
        def _(dve):
            dve.wait_ge(core.step.sem, core.step.n)
            dve.wait_ge(core.landed.sem, core.landed.n)
            dve.wait_ge(core.stored.sem, core.stored.n)
            for i in range(n):
                if who(i) == "v":
                    dve.wait_ge(core.filled.sem, f0 + i + 1)
                    take(dve, i, core.bank[i % BANKS]).then_inc(core.emptied_v.sem, core.emptied_v.one())

        @block.scalar
        def _(act):
            act.wait_ge(core.step.sem, core.step.n)
            act.wait_ge(core.landed.sem, core.landed.n)
            act.wait_ge(core.stored.sem, core.stored.n)
            for i in range(n):
                if who(i) == "s":
                    act.wait_ge(core.filled.sem, f0 + i + 1)
                    take(act, i, core.bank[i % BANKS]).then_inc(core.emptied_s.sem, core.emptied_s.one())


def copy(core, eng, dst, src):
    if eng is core.nc.scalar:
        return eng.activation(dst, src, ACT.Copy)
    return eng.tensor_copy(dst, src)


def turns(i):
    return "v" if i % 2 == 0 else "s"


def weight_load(slot, src, kt, c0, n):
    cols = src.shape[-1]
    return lambda sp: sp.dma_start(slot, dram(src, c0, [[cols, P], [P * cols, kt], [1, n]]))


def dense(core, xT, kt, tokens, w, c0, ncols, take, transposed=False, who=None, extra=None, width=512):
    chunks = -(-ncols // width)
    groups, first, last = [], {}, {}
    for c in range(chunks):
        n = min(width, ncols - c * width)
        first[c] = len(groups)
        if transposed:
            for s in range(0, n, P):
                for t0 in range(0, tokens, BANK):
                    groups.append((c, s, min(P, n - s), t0, min(BANK, tokens - t0)))
        else:
            for tt in range(tokens // P):
                groups.append((c, 0, n, tt, P))
        last[c] = len(groups) - 1
    with core.scope() as sb:
        ring = [sb("weights", [P, kt, width]) for _ in range(2)]

        def fill(pe, i, bank):
            c, s, n, t, m = groups[i]
            w_sb = ring[c % 2]
            for k in range(kt):
                if transposed:
                    ins = pe.matmul(bank[:n, :m], w_sb[:, k, s:s + n], xT[:, k, t:t + m],
                                    start=k == 0, stop=k == kt - 1)
                else:
                    ins = pe.matmul(bank[:, :n], xT[:, k, t * P:t * P + P], w_sb[:, k, :n],
                                    start=k == 0, stop=k == kt - 1)
            return ins

        def taken(eng, i, bank):
            c, s, n, t, m = groups[i]
            if transposed:
                return take(eng, (c * width + s) // P, t, m, bank[:n, :m])
            return take(eng, t, c * width, n, bank[:, :n])

        def load(sp, c):
            n = min(width, ncols - c * width)
            return [weight_load(ring[c % 2][:, :, :n], w, kt, c0 + c * width, n)(sp)]

        products(core, len(groups), fill, taken, who or turns, chunks, load,
                 lambda c: last[c], lambda c: first[c])


def transposes(core, jobs, ident, scale=None):
    def fill(pe, i, bank):
        off = 0
        for src in jobs[i][1]:
            p, f = src.shape[0], src.shape[1]
            ins = pe.transpose(bank[:f, off:off + p], src, ident[:p, :p])
            off += p
        return ins

    def take(eng, i, bank):
        dst, srcs = jobs[i][0], jobs[i][1]
        f, total = srcs[0].shape[1], sum(s.shape[0] for s in srcs)
        src = bank[:f, :total]
        if len(dst.shape) == 3:
            src = src.rearrange("p (a b) -> p a b", b=dst.shape[2])
        if len(dst.shape) == 4:
            src = src.rearrange("p (a b c) -> p a b c", b=dst.shape[2], c=dst.shape[3])
        return copy(core, eng, dst, src)

    products(core, len(jobs), fill, take, turns)


def rstd_of(core, ss, n, eps):
    dve, act = core.nc.vector, core.nc.scalar
    step, landed, stored = core.step, core.landed, core.stored
    dve.wait_ge(step.sem, step.n)
    dve.tensor_scalar(ss, ss, 1.0 / n, eps, ALU.mult, ALU.add).then_inc(step.sem, step.one())
    act.wait_ge(step.sem, step.n)
    act.activation(ss, ss, ACT.Sqrt).then_inc(step.sem, step.one())
    dve.wait_ge(step.sem, step.n)
    dve.reciprocal(ss, ss).then_inc(step.sem, step.one())


def rms_tokens(core, sb, x, out, nt, n, eps=EPS):
    dve, act = core.nc.vector, core.nc.scalar
    step, landed, stored = core.step, core.landed, core.stored
    ss = sb("square_sums", [P, nt])
    junk = sb("squares", [P, n])
    for t in range(nt):
        act.wait_ge(step.sem, step.n)
        act.wait_ge(landed.sem, landed.n)
        act.wait_ge(stored.sem, stored.n)
        act.activation(junk[:, :], x[:, t], ACT.Square, accum_out=ss[:, t:t + 1]).then_inc(step.sem, step.one())
    rstd_of(core, ss[:, :], n, eps)
    for t in range(nt):
        dve.wait_ge(step.sem, step.n)
        dve.tensor_scalar(out[:, t], x[:, t], ss[:, t:t + 1], None, ALU.mult).then_inc(step.sem, step.one())


def rms_heads(core, x, heads, n, gain, scale=1.0):
    dve, act = core.nc.vector, core.nc.scalar
    step, landed, stored = core.step, core.landed, core.stored
    with core.scope() as sb:
        sq = sb("squares", [P, heads, n])
        ss = sb("square_sums", [P, heads])
        act.wait_ge(step.sem, step.n)
        act.wait_ge(landed.sem, landed.n)
        act.wait_ge(stored.sem, stored.n)
        act.activation(sq[:, :, :], x, ACT.Square).then_inc(step.sem, step.one())
        dve.wait_ge(step.sem, step.n)
        dve.tensor_reduce(ss[:, :], sq[:, :, :], AX.X, ALU.add).then_inc(step.sem, step.one())
        rstd_of(core, ss[:, :], n, EPS)
        if scale != 1.0:
            dve.wait_ge(step.sem, step.n)
            dve.tensor_scalar(ss[:, :], ss[:, :], scale, None, ALU.mult).then_inc(step.sem, step.one())
        dve.wait_ge(step.sem, step.n)
        dve.tensor_tensor(x, x, bc(ss[:, :], n), ALU.mult).then_inc(step.sem, step.one())
        if gain is not None:
            dve.wait_ge(step.sem, step.n)
            dve.tensor_tensor(x, x, mid(gain, heads), ALU.mult).then_inc(step.sem, step.one())


def softmax_rows(core, s, rows, n, neg_max, den):
    dve, act = core.nc.vector, core.nc.scalar
    step, landed, stored = core.step, core.landed, core.stored
    dve.wait_ge(step.sem, step.n)
    dve.wait_ge(landed.sem, landed.n)
    dve.wait_ge(stored.sem, stored.n)
    dve.tensor_reduce(neg_max, s, AX.X, ALU.max).then_inc(step.sem, step.one())
    dve.wait_ge(step.sem, step.n)
    dve.tensor_scalar(neg_max, neg_max, -1.0, None, ALU.mult).then_inc(step.sem, step.one())
    for r in range(rows):
        act.wait_ge(step.sem, step.n)
        act.activation(s[:, r], s[:, r], ACT.Exp, bias=neg_max[:, r:r + 1],
                        accum_out=den[:, r:r + 1]).then_inc(step.sem, step.one())
    dve.wait_ge(step.sem, step.n)
    dve.reciprocal(den, den).then_inc(step.sem, step.one())



def t5_bucket(rel):
    half = BUCKETS // 2
    max_exact = half // 2
    n = np.abs(rel)
    large = max_exact + (np.log(np.maximum(n, 1) / max_exact)
                         / np.log(REL_MAX / max_exact) * (half - max_exact)).astype(np.int32)
    large = np.minimum(large, half - 1)
    return np.where(rel > 0, half, 0) + np.where(n < max_exact, n, large)


REL_N = 1024
REL_C = 511


def shape_constants():
    out = {}
    f = np.float32
    i = np.arange(P)
    out["ident"] = np.eye(P, dtype=f)
    onehot = np.zeros((NG, BUCKETS, REL_N), f)
    banned = np.zeros((NG, REL_N), f)
    rel = np.arange(REL_N) - REL_C
    for g, (window, dil) in enumerate(GROUPS):
        ok = (rel % dil == 0) & (np.abs(rel) <= (window // 2) // dil * dil)
        b = t5_bucket(rel)
        onehot[g, b[ok], np.nonzero(ok)[0]] = 1
        banned[g, ~ok] = NEG
    out["onehot"] = onehot
    out["banned"] = banned
    same = (i[:, None] // 32) == (i[None] // 32)
    s, t = i[:, None], i[None]
    tri = np.zeros((2, 3, P, P), f)
    for d in range(2):
        a, b = (s, t) if d == 0 else (t, s)
        tri[d, 0] = same & (a <= b)
        tri[d, 1] = same & (a > b)
        tri[d, 2] = same & (a < b)
    out["tri"] = tri
    same16 = (i[:, None] // 16) == (i[None] // 16)
    m = np.zeros((2, 4, P, P), np.int32)
    for d in range(2):
        a, b = (s, t) if d == 0 else (t, s)
        m[d, 0] = same & (a <= b)
        m[d, 1] = same & (a < b)
        m[d, 2] = same16 & (a < b)
        m[d, 3] = same & ~same16 & (a < b)
    out["masks"] = m
    out["masks_f"] = m.astype(f)
    blk = (i[:, None] // 64) == (i[None] // 64)
    out["ones"] = np.stack([np.ones((P, P), f), blk.astype(f)])
    tok = np.arange(SEQ)
    half = ROPE // 2
    inv = (f(10000.0) ** (-np.arange(0, half, 2, dtype=f) / f(half))).astype(f)
    ar = (tok // GRID_W).astype(f)[:, None] * inv
    ac = (tok % GRID_W).astype(f)[:, None] * inv
    ang = np.concatenate([ar, ar, ac, ac], -1)
    cos, sin = np.cos(ang).astype(f), np.sin(ang).astype(f)
    sgn = np.where((np.arange(ROPE) % half) < half // 2, -1, 1).astype(f)
    out["rope"] = np.stack([cos, sin * sgn])
    cols = np.arange(GRID_W)
    start = np.clip(cols - WIN_W // 2, 0, GRID_W - WIN_W)
    ok = (cols[None] >= start[:, None]) & (cols[None] < start[:, None] + WIN_W)
    win = np.where(ok, 0, NEG).astype(f)
    out["window"] = np.concatenate([win, win], 0)
    out["iota_row"] = np.arange(SEQ, dtype=f)[None]
    out["iota_col"] = (np.arange(NT)[None] * P + i[:, None]).astype(f)
    return out



def transpose_tokens(core, x, xT, nt, ident):
    kt = x.shape[2] // P
    jobs = []
    for k in range(kt):
        for t0 in range(0, nt, 4):
            m = min(4, nt - t0)
            jobs.append((xT[:, k, t0 * P:(t0 + m) * P], [x[:, t, k * P:k * P + P] for t in range(t0, t0 + m)]))
    transposes(core, jobs, ident)


def first_attention(core, I, C, hT, ya, scratch, copies):
    nc = core.nc
    dve, act = nc.vector, nc.scalar
    step, landed, stored = core.step, core.landed, core.stored
    NQ = NT * AH
    with core.scope() as sb:
        v = sb("v", [P, NG, NT, AW])
        o = sb("attended", [P, NT, AW])
        qkT = sb("qkT", [P, NG, 2, AH // 2, SEQ])
        gains = sb("gains", [P, NG, 2, HD])
        with core.scope() as sb2:
            table = sb2("table", [BUCKETS, NG * AH])
            onehot = sb2("onehot", [BUCKETS, NG, REL_N])
            banned = sb2("banned", [AH, NG, REL_N])
            vec = sb2("bias_of_distance", [AH, NG, REL_N])
            core.load(table[:, :], I["rel_bias"])
            core.load(onehot[:, :, :], I["onehot"].rearrange("g b n -> b g n"))
            for g in range(NG):
                core.load(banned[:, g], dram(I["banned"], g * REL_N, [[0, AH], [1, REL_N]]))

            def fill(pe, i, bank):
                g, c = i // 2, i % 2
                return pe.matmul(bank[:AH, :], table[:, g * AH:(g + 1) * AH],
                                 onehot[:, g, c * 512:c * 512 + 512], start=True, stop=True)

            def take(eng, i, bank):
                g, c = i // 2, i % 2
                s = slice(c * 512, c * 512 + 512)
                return eng.tensor_tensor(vec[:, g, s], bank[:AH, :], banned[:, g, s], ALU.add)

            products(core, 2 * NG, fill, take)
            core.store(scratch.rearrange("g h n -> h g n"), vec[:, :, :])
        for g in range(NG):
            load_rows(core, gains[:, g, 0], I["q_norm_w"], g * HD, HD)
            load_rows(core, gains[:, g, 1], I["k_norm_w"], g * HD, HD)
        with core.scope() as sb2:
            x = sb2("q_or_k", [P, NT, AW])
            for g in range(NG):
                for j in range(2):
                    dense(core, hT, KT, SEQ, I["w_in"], (g * 3 + j) * AW, AW,
                          lambda e, tt, col, n, ps: copy(core, e, x[:, tt, :], ps))
                    rms_heads(core, x[:, :, :].rearrange("p t (h n) -> p (t h) n", n=HD), NQ, HD,
                              gains[:, g, j], HD ** -0.5 if j == 0 else 1.0)
                    transpose_tokens(core, x, qkT[:, g, j], NT, C["ident"])
        for g in range(NG):
            dense(core, hT, KT, SEQ, I["w_in"], (g * 3 + 2) * AW, AW,
                  lambda e, tt, col, n, ps, g=g: copy(core, e, v[:, g, tt, :], ps))
        with core.scope() as sb2:
            s = sb2("scores", [P, NT, NG * SEQ])
            pT = sb2("weightsT", [P, NG * NT, SEQ])
            bias = sb2("bias", [P, NG, 896])
            neg_max = sb2("neg_max", [P, NT])
            den = sb2("den", [P, NT])
            for h in range(AH):
                for g in range(NG):
                    core.store(dram(copies, g * P * REL_N, [[REL_N, P], [1, REL_N]]),
                               dram(scratch, (g * AH + h) * REL_N, [[0, P], [1, REL_N]]))
                for g in range(NG):
                    core.load(bias[:, g, :], dram(copies, g * P * REL_N + REL_C - 384, [[REL_N - 1, P], [1, 896]]))
                lo = (h % 2) * HD

                def fill(pe, i, bank):
                    t, g = i // NG, i % NG
                    return pe.matmul(bank[:, :], qkT[lo:lo + HD, g, 0, h // 2, t * P:t * P + P],
                                     qkT[lo:lo + HD, g, 1, h // 2, :], start=True, stop=True)

                def take(eng, i, bank):
                    t, g = i // NG, i % NG
                    c = 384 - t * P
                    return eng.tensor_tensor(s[:, t, g * SEQ:(g + 1) * SEQ], bank[:, :],
                                             bias[:, g, c:c + SEQ], ALU.add)

                products(core, NT * NG, fill, take)
                softmax_rows(core, s[:, :, :], NT, NG * SEQ, neg_max[:, :], den[:, :])
                transposes(core, [(pT[:, kk, :], [s[:, t, kk * P:kk * P + P] for t in range(NT)])
                                  for kk in range(NG * NT)], C["ident"])

                def fill(pe, t, bank):
                    for kk in range(NG * NT):
                        ins = pe.matmul(bank[:, :HD], pT[:, kk, t * P:t * P + P],
                                        v[:, kk // NT, kk % NT, h * HD:(h + 1) * HD],
                                        start=kk == 0, stop=kk == NG * NT - 1)
                    return ins

                products(core, NT, fill, lambda e, t, bank: e.tensor_scalar(
                    o[:, t, h * HD:(h + 1) * HD], bank[:, :HD], den[:, t:t + 1], None, ALU.mult))
        with core.scope() as sb2:
            gate = sb2("gate", [P, NT, AW])
            dense(core, hT, KT, SEQ, I["w_in"], OFF_GA, AW,
                  lambda e, tt, col, n, ps: e.activation(gate[:, tt, :], ps, ACT.Silu), who=lambda i: "s")
            dve.wait_ge(step.sem, step.n)
            dve.tensor_tensor(o[:, :, :], o[:, :, :], gate[:, :, :], ALU.mult).then_inc(step.sem, step.one())
            oT = sb2("attendedT", [P, AW // P, SEQ])
            transpose_tokens(core, o, oT, NT, C["ident"])
            dense(core, oT, AW // P, SEQ, I["w_proj_a"], 0, D,
                  lambda e, tt, col, n, ps: copy(core, e, ya[:, tt, col:col + n], ps))


def gated_recurrence(core, I, C, hT, oT):
    nc = core.nc
    dve, act = nc.vector, nc.scalar
    step, landed, stored = core.step, core.landed, core.stored
    CH = GLA_CHUNK
    NCH = SEQ // CH
    HB = 4
    with core.scope() as sb:
        qT = sb("qT", [P, HH, SEQ])
        v = sb("values", [P, NT, D])
        tri = sb("sums_in_chunk", [P, 2, 2, P])
        lower = sb("causal_in_chunk", [P, 2, P], I32)
        for kind in range(2):
            core.load(tri[:, :, kind], dram(I["tri"], kind * P * P, [[P, P], [3 * P * P, 2], [1, P]]))
        core.load(lower[:, :, :], dram(I["masks"], 0, [[P, P], [4 * P * P, 2], [1, P]]))
        z = sb("log_decay", [P, NT, D])
        k = sb("keys", [P, NT, D])
        dense(core, hT, KT, SEQ, I["w_in"], OFF_Q, D,
              lambda e, ct, t0, n, ps: copy(core, e, qT[:, ct, t0:t0 + n], ps), transposed=True, width=256)
        dense(core, hT, KT, SEQ, I["w_in"], OFF_I, D,
              lambda e, tt, col, n, ps: copy(core, e, v[:, tt, col:col + n], ps), width=256)
        for d in range(2):
            with core.scope() as sb2:
                lb = sb2("lower_bound", [P, D])
                one_lb = sb2("one_minus_lower_bound", [P, D])
                src = I["lb_bwd"] if d else I["lb_fwd"]
                load_rows(core, lb[:, :], src, 0, D)
                load_rows(core, one_lb[:, :], src, D, D)
                with core.scope() as sb3:
                    top = sb3("top", [P, D])
                    dve.wait_ge(step.sem, step.n)
                    dve.wait_ge(landed.sem, landed.n)
                    dve.wait_ge(stored.sem, stored.n)
                    dve.tensor_tensor(top[:, :], lb[:, :], one_lb[:, :], ALU.max).then_inc(step.sem, step.one())
                    dve.wait_ge(step.sem, step.n)
                    dve.tensor_tensor(lb[:, :], lb[:, :], top[:, :], ALU.subtract).then_inc(step.sem, step.one())
                    dve.wait_ge(step.sem, step.n)
                    dve.tensor_tensor(one_lb[:, :], one_lb[:, :], top[:, :], ALU.subtract).then_inc(step.sem, step.one())
                    act.wait_ge(step.sem, step.n)
                    act.activation(lb[:, :], lb[:, :], ACT.Exp).then_inc(step.sem, step.one())
                    act.wait_ge(step.sem, step.n)
                    act.activation(one_lb[:, :], one_lb[:, :], ACT.Exp).then_inc(step.sem, step.one())
                    dve.wait_ge(step.sem, step.n)
                    dve.tensor_tensor(top[:, :], lb[:, :], one_lb[:, :], ALU.add).then_inc(step.sem, step.one())
                    dve.wait_ge(step.sem, step.n)
                    dve.reciprocal(top[:, :], top[:, :]).then_inc(step.sem, step.one())
                    dve.wait_ge(step.sem, step.n)
                    dve.tensor_tensor(lb[:, :], lb[:, :], top[:, :], ALU.mult).then_inc(step.sem, step.one())
                    dve.wait_ge(step.sem, step.n)
                    dve.tensor_scalar(one_lb[:, :], lb[:, :], -1.0, 1.0, ALU.mult, ALU.add).then_inc(step.sem, step.one())
                dense(core, hT, KT, SEQ, I["w_in"], OFF_ZB if d else OFF_ZF, D,
                      lambda e, tt, col, n, ps: e.activation(z[:, tt, col:col + n], ps, ACT.Sigmoid),
                      who=lambda i: "s", width=256)
                dve.wait_ge(step.sem, step.n)
                dve.tensor_tensor(z[:, :, :], z[:, :, :], mid(one_lb[:, :], NT), ALU.mult).then_inc(step.sem, step.one())
                dve.wait_ge(step.sem, step.n)
                dve.tensor_tensor(z[:, :, :], z[:, :, :], mid(lb[:, :], NT), ALU.add).then_inc(step.sem, step.one())
                dve.wait_ge(step.sem, step.n)
                dve.tensor_scalar(k[:, :, :], z[:, :, :], -1.0, 1.0, ALU.mult, ALU.add).then_inc(step.sem, step.one())
                act.wait_ge(step.sem, step.n)
                act.activation(z[:, :, :], z[:, :, :], ACT.Ln).then_inc(step.sem, step.one())
            for h0 in range(0, HH, HB):
                with core.scope() as sb2:
                    cum = sb2("exp_cumulative", [P, HB, SEQ])
                    qt = sb2("queries_scaled", [P, HB, SEQ])
                    ks = sb2("keys_to_end", [P, NT, HB * P])
                    aT = sb2("scoresT", [P, HB, NT, P])
                    room = sb2("keys_then_states", [P, NCH * HB * P])
                    kt = room[:, 0:HB * SEQ].rearrange("p (h t) -> p h t", h=HB)
                    hist = room[:, :].rearrange("p (c h n) -> p c h n", h=HB, n=P)
                    hc = h0 * P
                    transposes(core, [(kt[:, hh, :], [k[:, t, hc + hh * P:hc + hh * P + P] for t in range(NT)])
                                      for hh in range(HB)], C["ident"])

                    def fill(pe, i, bank):
                        for t in range(NT):
                            ins = pe.matmul(bank[:, t * P:t * P + P], z[:, t, hc + i * P:hc + i * P + P],
                                            tri[:, d, 0, :], start=True, stop=True)
                        return ins

                    def take(act, i, bank):
                        act.activation(cum[:, i, :], bank[:, :], ACT.Exp)
                        return act.activation(qt[:, i, :], bank[:, :], ACT.Exp, scale=-1.0)

                    products(core, HB, fill, take, lambda i: "s")
                    dve.wait_ge(step.sem, step.n)
                    dve.tensor_tensor(kt, kt, qt[:, :, :], ALU.mult).then_inc(step.sem, step.one())
                    dve.wait_ge(step.sem, step.n)
                    dve.tensor_tensor(qt[:, :, :], qT[:, h0:h0 + HB, :], cum[:, :, :], ALU.mult).then_inc(step.sem, step.one())

                    def fill(pe, t, bank):
                        return pe.matmul(bank[:, :], tri[:, d, 1, :], z[:, t, hc:hc + HB * P],
                                         start=True, stop=True)

                    products(core, NT, fill, lambda e, t, bank: e.activation(ks[:, t, :], bank[:, :], ACT.Exp),
                             lambda i: "s")
                    dve.wait_ge(step.sem, step.n)
                    dve.tensor_tensor(ks[:, :, :], ks[:, :, :], k[:, :, hc:hc + HB * P], ALU.mult).then_inc(step.sem, step.one())
                    dve.wait_ge(step.sem, step.n)
                    dve.memset(aT[:, :, :, :], 0.0).then_inc(step.sem, step.one())

                    def fill(pe, i, bank):
                        for t in range(NT):
                            ins = pe.matmul(bank[:, t * P:t * P + P], kt[:, i, t * P:t * P + P],
                                            qt[:, i, t * P:t * P + P], start=True, stop=True)
                        return ins

                    products(core, HB, fill, lambda e, i, bank: e.copy_predicated(
                        aT[:, i, :, :], mid(lower[:, d, :], NT),
                        bank[:, :].rearrange("p (t n) -> p t n", t=NT)))
                    order = list(range(NCH)) if d == 0 else list(range(NCH - 1, -1, -1))
                    edge = CH - 1 if d == 0 else 0
                    dve.wait_ge(step.sem, step.n)
                    dve.memset(hist[:, order[0], :, :], 0.0).then_inc(step.sem, step.one())

                    def fill(pe, i, bank):
                        c = order[i]
                        r = slice((c % 4) * CH, (c % 4) * CH + CH)
                        for hh in range(HB):
                            ins = pe.matmul(bank[:, hh * P:hh * P + P], ks[r, c // 4, hh * P:hh * P + P],
                                            v[r, c // 4, hc + hh * P:hc + hh * P + P], start=True, stop=True)
                        return ins

                    def take(eng, i, bank):
                        c, nxt = order[i], order[i + 1]
                        eng.wait_ge(core.emptied_v.sem, core.emptied_v.n)
                        for hh in range(HB):
                            ins = eng.scalar_tensor_tensor(
                                out=hist[:, nxt, hh, :], in0=hist[:, c, hh, :],
                                scalar=cum[:, hh, c * CH + edge:c * CH + edge + 1],
                                in1=bank[:, hh * P:hh * P + P], op0=ALU.mult, op1=ALU.add)
                        return ins

                    products(core, NCH - 1, fill, take)

                    def fill(pe, i, bank):
                        for t in range(NT):
                            pe.matmul(bank[:, t * P:t * P + P], v[:, t, hc + i * P:hc + i * P + P],
                                      aT[:, i, t, :], start=t == 0, stop=False)
                        for c in range(NCH):
                            ins = pe.matmul(bank[:, c * CH:c * CH + CH], hist[:, c, i, :],
                                            qt[:, i, c * CH:c * CH + CH], start=False, stop=c == NCH - 1)
                        return ins

                    if d == 0:
                        take = lambda e, i, bank: e.tensor_copy(oT[:, h0 + i, :], bank[:, :])
                    else:
                        take = lambda e, i, bank: e.tensor_tensor(oT[:, h0 + i, :], oT[:, h0 + i, :],
                                                                  bank[:, :], ALU.add)
                    products(core, HB, fill, take)


def first_block(core, I, C, X, scratch, copies):
    nc = core.nc
    dve, act = nc.vector, nc.scalar
    step, landed, stored = core.step, core.landed, core.stored
    with core.scope() as sb:
        hT = sb("hT", [P, KT, SEQ])
        ya = sb("attention_out", [P, NT, D])
        with core.scope() as sb2:
            h = sb2("h", [P, NT, D])
            w = sb2("norm_w", [P, D])
            load_rows(core, w[:, :], I["norm_w"], 0, D)
            rms_tokens(core, sb2, X, h, NT, D)
            dve.wait_ge(step.sem, step.n)
            dve.wait_ge(landed.sem, landed.n)
            dve.wait_ge(stored.sem, stored.n)
            dve.tensor_tensor(h[:, :, :], h[:, :, :], mid(w[:, :], NT), ALU.mult).then_inc(step.sem, step.one())
            transpose_tokens(core, h, hT, NT, C["ident"])
        first_attention(core, I, C, hT, ya, scratch, copies)
        with core.scope() as sb2:
            oT = sb2("recurrentT", [P, HH, SEQ])
            gated_recurrence(core, I, C, hT, oT)
            with core.scope() as sb3:
                sq = sb3("squares", [P, HH, SEQ])
                gb = sb3("gateT", [P, HH, SEQ])
                w = sb3("gain", [P, 1])
                load_columns(core, w[:, :], I["hg_norm_w"], 0, 1)
                act.wait_ge(step.sem, step.n)
                act.wait_ge(landed.sem, landed.n)
                act.wait_ge(stored.sem, stored.n)
                act.activation(sq[:, :, :], oT[:, :, :], ACT.Square).then_inc(step.sem, step.one())
                products(core, HH, lambda pe, i, bank: pe.matmul(bank[:, :], C["ones"][:, 0, :], sq[:, i, :],
                                                                 start=True, stop=True),
                         lambda e, i, bank: e.tensor_scalar(gb[:, i, :], bank[:, :], 1.0 / HDK, EPS,
                                                            ALU.mult, ALU.add))
                act.wait_ge(step.sem, step.n)
                act.activation(gb[:, :, :], gb[:, :, :], ACT.Sqrt).then_inc(step.sem, step.one())
                dve.wait_ge(step.sem, step.n)
                dve.reciprocal(gb[:, :, :], gb[:, :, :]).then_inc(step.sem, step.one())
                dve.wait_ge(step.sem, step.n)
                dve.tensor_tensor(oT[:, :, :], oT[:, :, :], gb[:, :, :], ALU.mult).then_inc(step.sem, step.one())
                dve.wait_ge(step.sem, step.n)
                dve.tensor_scalar(oT[:, :, :], oT[:, :, :], w[:, 0:1], None, ALU.mult).then_inc(step.sem, step.one())
                dense(core, hT, KT, SEQ, I["w_in"], OFF_GB, D,
                      lambda e, ct, t0, n, ps: e.activation(gb[:, ct, t0:t0 + n], ps, ACT.Silu),
                      transposed=True, who=lambda i: "s")
                dve.wait_ge(step.sem, step.n)
                dve.tensor_tensor(oT[:, :, :], oT[:, :, :], gb[:, :, :], ALU.mult).then_inc(step.sem, step.one())
            with core.scope() as sb3:
                yb = sb3("recurrence_out", [P, NT, D])
                dense(core, oT, HH, SEQ, I["w_proj_b"], 0, D,
                      lambda e, tt, col, n, ps: copy(core, e, yb[:, tt, col:col + n], ps))
                g = sb3("gate", [P, NT, D])
                for off, y in ((OFF_ZGA, ya), (OFF_ZGB, yb)):
                    dense(core, hT, KT, SEQ, I["w_in"], off, D,
                          lambda e, tt, col, n, ps: e.activation(g[:, tt, col:col + n], ps, ACT.Sigmoid),
                          who=lambda i: "s")
                    dve.wait_ge(step.sem, step.n)
                    dve.tensor_tensor(y[:, :, :], y[:, :, :], g[:, :, :], ALU.mult).then_inc(step.sem, step.one())
                dve.wait_ge(step.sem, step.n)
                dve.tensor_tensor(ya[:, :, :], ya[:, :, :], yb[:, :, :], ALU.add).then_inc(step.sem, step.one())
            transpose_tokens(core, ya, oT, NT, C["ident"])
            dense(core, oT, KT, SEQ, I["w_out"], 0, D,
                  lambda e, tt, col, n, ps: e.tensor_tensor(X[:, tt, col:col + n], X[:, tt, col:col + n],
                                                            ps, ALU.add), who=lambda i: "v")



SH1, SC1, G1, SH2, SC2, G2 = range(6)
MOD = 6 * D


def modulation(core, I, C, mod_dram):
    nc = core.nc
    dve, act = nc.vector, nc.scalar
    step, landed, stored = core.step, core.landed, core.stored
    W = BANK
    per = MOD // W
    with core.scope() as sb:
        rows = sb("conditions", [2 * KT, P])
        cT = sb("conditionsT", [P, 2 * KT])
        mod = sb("mod", [2, 2, MOD])
        bias = sb("bias", [2, 2, MOD])
        ring = [sb("weights", [P, KT, W]) for _ in range(2)]
        core.load(rows[0:KT, :], I["c_2"].rearrange("b (k p) -> (b k) p", p=P))
        core.load(rows[KT:2 * KT, :], I["c_ctx_2"].rearrange("(k p) -> k p", p=P))
        for i in range(2):
            core.load(bias[:, i, :], dram(I["ada_b_2"], i * MOD, [[0, 2], [1, MOD]]))
        act.wait_ge(step.sem, step.n)
        act.wait_ge(landed.sem, landed.n)
        act.wait_ge(stored.sem, stored.n)
        act.activation(rows[:, :], rows[:, :], ACT.Silu).then_inc(step.sem, step.one())
        transposes(core, [(cT[:, :], [rows[:, :]])], C["ident"])
        cv = cT[:, :].rearrange("p (w k) -> p k w", w=2)

        def fill(pe, i, bank):
            for k in range(KT):
                ins = pe.matmul(bank[:2, :], cv[:, k, :], ring[i % 2][:, k, :], start=k == 0, stop=k == KT - 1)
            return ins

        def take(eng, i, bank):
            s = slice(i % per * W, i % per * W + W)
            return eng.tensor_tensor(mod[:, i // per, s], bank[:2, :], bias[:, i // per, s], ALU.add)

        def load(sp, c):
            return [weight_load(ring[c % 2][:, :, :], I["ada_w_2"][c // per], KT, c % per * W, W)(sp)]

        products(core, 2 * per, fill, take, None, 2 * per, load, lambda c: c, lambda c: c)
        core.store(mod_dram.rearrange("l w n -> w l n"), mod[:, :, :])


def modulation_columns(core, C, mod_dram, layer, cols):
    with core.scope() as sb:
        rows = sb("mod_rows", [2 * 6 * KT, P])
        core.load(rows[:, :], mod_dram[layer].rearrange("w (j p) -> (w j) p", p=P))
        transposes(core, [(cols, [rows[:, :]])], C["ident"])


def norm_scales(core, cols, norm_g, layer, sc, scale):
    dve = core.nc.vector
    step, landed, stored = core.step, core.landed, core.stored
    with core.scope() as sb:
        g = sb("norm_gain", [P, KT])
        load_columns(core, g[:, :], norm_g, layer * D, KT)
        dve.wait_ge(step.sem, step.n)
        dve.wait_ge(landed.sem, landed.n)
        dve.wait_ge(stored.sem, stored.n)
        dve.tensor_scalar(scale, cols[:, :, sc, :], 1.0, None, ALU.add).then_inc(step.sem, step.one())
        dve.wait_ge(step.sem, step.n)
        dve.tensor_tensor(scale, scale, mid(g[:, :], 2), ALU.mult).then_inc(step.sem, step.one())


def modulated(core, xn, hT, scale, cols, sh, ident, nx=NX):
    jobs = []
    for k in range(KT):
        jobs.append((k, 0, 0, NT))
        if nx > NT:
            jobs.append((k, 1, NT, NX))

    def fill(pe, i, bank):
        k, w, a, b = jobs[i]
        for t in range(a, b):
            ins = pe.transpose(bank[:, (t - a) * P:(t - a) * P + P], xn[:, t, k * P:k * P + P], ident[:, :])
        return ins

    def take(eng, i, bank):
        k, w, a, b = jobs[i]
        return eng.tensor_scalar(hT[:, k, a * P:b * P], bank[:, :(b - a) * P], scale[:, w, k:k + 1],
                                 cols[:, w, sh, k:k + 1], ALU.mult, ALU.add)

    products(core, len(jobs), fill, take)


def gated_output(core, catT, w, X, mod_dram, layer, tokens):
    dve = core.nc.vector
    step, landed, stored = core.step, core.landed, core.stored
    nt = tokens // P
    with core.scope() as sb:
        y = sb("mixed", [P, nt, D])
        g = sb("gate_rows", [P, 2, D])
        for which in range(2):
            load_rows(core, g[:, which, :], mod_dram, (layer * 2 + which) * MOD + G1 * D, D)
        dense(core, catT, KT, tokens, w, 0, D,
              lambda e, tt, col, n, ps: e.tensor_tensor(y[:, tt, col:col + n], ps,
                                                        g[:, tt // NT, col:col + n], ALU.mult),
              who=lambda i: "v")
        dve.wait_ge(step.sem, step.n)
        dve.tensor_tensor(X[:, 0:nt], X[:, 0:nt], y[:, :, :], ALU.add).then_inc(step.sem, step.one())



def route(core, I, C, X, layer, nx, cols, sel_dram, xs):
    nc = core.nc
    dve, act = nc.vector, nc.scalar
    step, landed, stored = core.step, core.landed, core.stored
    parts = [(0, 0, NT, CAP_X)] + ([(1, NT, NX, CAP_C)] if nx > NT else [])
    with core.scope() as sb:
        xn = sb("normed", [P, nx, D])
        scale = sb("scale", [P, 2, KT])
        rms_tokens(core, sb, X, xn, nx, D)
        norm_scales(core, cols, I["norm2_g_2"], layer, SC2, scale[:, :, :])
        logits = sb("affinity", [P, nx, NE])
        with core.scope() as sb2:
            hT = sb2("hT", [P, KT, nx * P])
            router = sb2("router", [P, KT, NE])
            core.load(router[:, :, :], I["moe_router_2"][layer].rearrange("(k p) e -> p k e", p=P))
            modulated(core, xn, hT, scale, cols, SH2, C["ident"], nx)

            def fill(pe, t, bank):
                for k in range(KT):
                    ins = pe.matmul(bank[:, :NE], hT[:, k, t * P:t * P + P], router[:, k, :],
                                    start=k == 0, stop=k == KT - 1)
                return ins

            products(core, nx, fill, lambda e, t, bank: e.tensor_copy(logits[:, t, :], bank[:, :NE]))
        top = sb("row_max", [P, nx])
        dve.wait_ge(step.sem, step.n)
        dve.tensor_reduce(top[:, :], logits[:, :, :], AX.X, ALU.max).then_inc(step.sem, step.one())
        dve.wait_ge(step.sem, step.n)
        dve.tensor_tensor(logits[:, :, :], logits[:, :, :], bc(top[:, :], NE), ALU.subtract).then_inc(step.sem, step.one())
        act.wait_ge(step.sem, step.n)
        act.activation(logits[:, :, :], logits[:, :, :], ACT.Exp).then_inc(step.sem, step.one())
        dve.wait_ge(step.sem, step.n)
        dve.tensor_reduce(top[:, :], logits[:, :, :], AX.X, ALU.add).then_inc(step.sem, step.one())
        dve.wait_ge(step.sem, step.n)
        dve.reciprocal(top[:, :], top[:, :]).then_inc(step.sem, step.one())
        dve.wait_ge(step.sem, step.n)
        dve.tensor_tensor(logits[:, :, :], logits[:, :, :], bc(top[:, :], NE), ALU.mult).then_inc(step.sem, step.one())
        aff = sb("affinity_by_expert", [NE, nx * P])
        transposes(core, [(aff[:, a * P:b * P], [logits[:, t, :] for t in range(a, b)]) for _, a, b, _ in parts],
                   C["ident"])
        slots = [NE * cap for *_, cap in parts]
        gates = sb("gates", [NE, CAP_X + CAP_C])
        index = sb("index", [NE, CAP_X + CAP_C], U32)
        number = sb("number", [NE, CAP_X + CAP_C])
        off = 0
        for w, a, b, cap in parts:
            part = aff[:, a * P:b * P]
            for r in range(off, off + cap, 8):
                dve.wait_ge(step.sem, step.n)
                dve.max(gates[:, r:r + 8], part).then_inc(step.sem, step.one())
                dve.wait_ge(step.sem, step.n)
                dve.max_index(index[:, r:r + 8], gates[:, r:r + 8], part).then_inc(step.sem, step.one())
                dve.wait_ge(step.sem, step.n)
                dve.match_replace(part, gates[:, r:r + 8], part, -1.0).then_inc(step.sem, step.one())
            dve.wait_ge(step.sem, step.n)
            dve.tensor_copy(number[:, off:off + cap], index[:, off:off + cap]).then_inc(step.sem, step.one())
            for j, src in ((0, number), (1, gates)):
                core.store(dram(sel_dram, (j * 2 + w) * NE * CAP_X, [[cap, NE], [1, cap]]), src[:, off:off + cap])
            off += cap
        with core.scope() as sb2:
            iota = sb2("iota", [P, NT])
            core.load(iota[:, :], I["iota_col"])
            off = 0
            for w, a, b, cap in parts:
                with core.scope() as sb3:
                    n = NE * cap
                    row = sb3("slot_tokens", [P, n])
                    pick = sb3("pick", [P, b - a, n])
                    load_rows(core, row[:, :], sel_dram, w * NE * CAP_X, n)
                    for t in range(b - a):
                        dve.wait_ge(step.sem, step.n)
                        dve.wait_ge(landed.sem, landed.n)
                        dve.wait_ge(stored.sem, stored.n)
                        dve.tensor_scalar(pick[:, t, :], row[:, :], iota[:, t:t + 1], None, ALU.is_equal).then_inc(step.sem, step.one())
                    per = n // BANK
                    ne = BANK // cap

                    def fill(pe, i, bank):
                        k, c = i // per, i % per
                        for t in range(b - a):
                            ins = pe.matmul(bank[:, :], xn[:, a + t, k * P:k * P + P],
                                            pick[:, t, c * BANK:c * BANK + BANK], start=t == 0, stop=t == b - a - 1)
                        return ins

                    def take(eng, i, bank):
                        k, c = i // per, i % per
                        return eng.tensor_scalar(xs[:, k, c * ne:(c + 1) * ne, off:off + cap],
                                                 bank[:, :].rearrange("p (e s) -> p e s", s=cap),
                                                 scale[:, w, k:k + 1], cols[:, w, SH2, k:k + 1], ALU.mult, ALU.add)

                    products(core, KT * per, fill, take)
                off += cap


def experts(core, I, C, X, layer, nx, mod_dram, sel_dram, xs):
    nc = core.nc
    with_ctx = nx > NT
    S = CAP_X + (CAP_C if with_ctx else 0)
    RING = 6
    HALF = D // 2
    sem = [Signal(nc, f"expert_weights_{layer}_{r}") for r in range(RING)]
    hid_filled, silu_done, hid_done = (Signal(nc, f"{n}_{layer}") for n in ("hidden_filled", "silu_done", "hidden_done"))
    out_filled, out_taken = (Signal(nc, f"{n}_{layer}") for n in ("out_filled", "out_taken"))
    place_ready, add_filled, add_done = (Signal(nc, f"{n}_{layer}") for n in ("place_ready", "add_filled", "add_done"))
    with core.scope() as sb:
        ring = [sb("expert_weights", [P, KT, HALF]) for _ in range(RING)]
        hid = sb("hidden", [P, 2, KT, S])
        act_out = sb("silu", [P, 3, S])
        ys = sb("outputs", [P, 2, D])
        ysc = sb("context_outputs", [P, D])
        place = sb("place", [P, 2, SEQ])
        placec = sb("context_place", [P, CTX])
        g2 = sb("gate_rows", [S, D])
        gate = sb("gates", [S, NE])
        num = sb("numbers", [P, NE // 2 + NE // 4])
        iota = sb("iota_row", [P, SEQ])
        load_rows(core, iota[:, :], I["iota_row"], 0, SEQ)
        for w in range(2 if with_ctx else 1):
            a, cap, q = (0, CAP_X, NE // 2) if w == 0 else (CAP_X, CAP_C, NE // 4)
            core.load(g2[a:a + cap, :], dram(mod_dram, (layer * 2 + w) * MOD + G2 * D, [[0, cap], [1, D]]))
            core.load(gate[a:a + cap, :], dram(sel_dram, (2 + w) * NE * CAP_X, [[1, cap], [cap, NE]]))
            core.load(num[:, w * (NE // 2):w * (NE // 2) + q], dram(sel_dram, w * NE * CAP_X, [[1, P], [P, q]]))
        names = ("moe_w1_2", "moe_w3_2")
        plan = [(names[m % 2], m // 2) for m in range(4)] + [("moe_w2_2", m) for m in range(2)]
        GRP = 8
        adds = [(q, t, h) for q in range(NE // 2) for t in range(NT) for h in range(2)]
        order = []
        for q in range(NE // 2):
            order.append([("x", q, t, h) for t in range(NT) for h in range(2)]
                         + ([("c", q // 2, t, h) for t in range(NC) for h in range(2)] if with_ctx and q % 2 else []))
        before = [sum(len(o) for o in order[:q]) for q in range(len(order) + 1)]

        with nc.Block() as block:
            @block.sync
            def _(sp):
                sp.wait_ge(core.step.sem, core.step.n)
                sp.wait_ge(core.landed.sem, core.landed.n)
                sp.wait_ge(core.stored.sem, core.stored.n)
                for n in range(6 * NE):
                    e, m = n // 6, n % 6
                    if n >= RING:
                        if m < 4:
                            sp.wait_ge(hid_filled.sem, (e - 1) * GRP + (m // 2 + 1) * 4)
                        else:
                            sp.wait_ge(out_filled.sem, (e - 1) * 2 + m - 3)
                    name, h = plan[m]
                    src = I[name][layer, e]
                    eng_ins = sp.dma_start(ring[n % RING][:, :, :], dram(src, h * HALF, [[D, P], [P * D, KT], [1, HALF]]))
                    eng_ins.then_inc(sem[n % RING].sem, sem[n % RING].sixteen())

            def landed(pe, e, m):
                n = e * 6 + m
                pe.wait_ge(sem[n % RING].sem, 16 * (n // RING + 1))

            @block.tensor
            def _(pe):
                pe.wait_ge(core.step.sem, core.step.n)
                pe.wait_ge(core.landed.sem, core.landed.n)
                pe.wait_ge(core.stored.sem, core.stored.n)

                def hidden(e):
                    for f in range(GRP):
                        h, g = f // 4, e * GRP + f
                        if f % 4 == 0:
                            landed(pe, e, 2 * h)
                            landed(pe, e, 2 * h + 1)
                        if g >= 3:
                            pe.wait_ge(hid_done.sem, g - 2)
                        bank = core.bank[g % 3]
                        for m in range(2):
                            w = ring[(e * 6 + 2 * h + m) % RING]
                            for k in range(KT):
                                ins = pe.matmul(bank[:, m * 256:m * 256 + S], w[:, k, (f % 4) * P:(f % 4) * P + P],
                                                xs[:, k, e, 0:S], start=k == 0, stop=k == KT - 1)
                        ins.then_inc(hid_filled.sem, hid_filled.one())

                def output(e):
                    pe.wait_ge(hid_done.sem, (e + 1) * GRP)
                    for h in range(2):
                        landed(pe, e, 4 + h)
                        g = 2 * e + h
                        if g >= 2:
                            pe.wait_ge(out_taken.sem, g - 1)
                        w = ring[(e * 6 + 4 + h) % RING]
                        for f in range(KT):
                            ins = pe.matmul(core.bank[3 + h][:S, :], hid[:, e % 2, f, :], w[:, f, :],
                                            start=f == 0, stop=f == KT - 1)
                        ins.then_inc(out_filled.sem, out_filled.one())

                def additions(q):
                    pe.wait_ge(out_taken.sem, 4 * q + 4)
                    pe.wait_ge(place_ready.sem, q + 1)
                    for i, (kind, j, t, h) in enumerate(order[q]):
                        n = before[q] + i
                        if n >= 3:
                            pe.wait_ge(add_done.sem, n - 2)
                        src, at = (ys[:, j % 2, :], place[:, j % 2, :]) if kind == "x" else (ysc[:, :], placec[:, :])
                        pe.matmul(core.bank[5 + n % 3][:, :], at[:, t * P:t * P + P],
                                                src[:, h * HALF:h * HALF + HALF], start=True, stop=True).then_inc(add_filled.sem, add_filled.one())

                for e in range(NE):
                    hidden(e)
                    if e % 2 == 0 and e:
                        additions(e // 2 - 1)
                    output(e)
                additions(NE // 2 - 1)

            @block.scalar
            def _(act):
                act.wait_ge(core.step.sem, core.step.n)
                act.wait_ge(core.landed.sem, core.landed.n)
                act.wait_ge(core.stored.sem, core.stored.n)
                for g in range(NE * GRP):
                    act.wait_ge(hid_filled.sem, g + 1)
                    if g >= 3:
                        act.wait_ge(hid_done.sem, g - 2)
                    act.activation(act_out[:, g % 3, :], core.bank[g % 3][:, 0:S], ACT.Silu).then_inc(silu_done.sem, silu_done.one())

            @block.vector
            def _(dve):
                dve.wait_ge(core.step.sem, core.step.n)
                dve.wait_ge(core.landed.sem, core.landed.n)
                dve.wait_ge(core.stored.sem, core.stored.n)

                def hidden(e):
                    for f in range(GRP):
                        g = e * GRP + f
                        if e >= 2 and f == 0:
                            dve.wait_ge(out_filled.sem, 2 * (e - 1))
                        dve.wait_ge(silu_done.sem, g + 1)
                        dve.tensor_tensor(hid[:, e % 2, f, :], act_out[:, g % 3, :],
                                                      core.bank[g % 3][:, 256:256 + S], ALU.mult).then_inc(hid_done.sem, hid_done.one())

                def places(q):
                    if q >= 2:
                        dve.wait_ge(add_filled.sem, before[q - 1])
                    ins = dve.tensor_scalar(place[:, q % 2, :], iota[:, :], num[:, q:q + 1], None, ALU.is_equal)
                    if with_ctx and q % 2:
                        if q >= 2:
                            dve.wait_ge(add_filled.sem, before[q - 1])
                        ins = dve.tensor_scalar(placec[:, :], iota[:, :CTX], num[:, NE // 2 + q // 2:NE // 2 + q // 2 + 1],
                                                None, ALU.is_equal)
                    ins.then_inc(place_ready.sem, place_ready.one())

                def output(e):
                    q = e // 2
                    if e % 2 == 0:
                        places(q)
                    if with_ctx and e % 4 == 0 and e:
                        dve.wait_ge(add_filled.sem, before[q])
                    for h in range(2):
                        s = slice(h * HALF, h * HALF + HALF)
                        bank = core.bank[3 + h]
                        dve.wait_ge(out_filled.sem, 2 * e + h + 1)
                        r = (e % 2) * CAP_X
                        ins = dve.scalar_tensor_tensor(out=ys[r:r + CAP_X, q % 2, s], in0=bank[0:CAP_X, :],
                                                       scalar=gate[0:CAP_X, e:e + 1], in1=g2[0:CAP_X, s],
                                                       op0=ALU.mult, op1=ALU.mult)
                        if with_ctx:
                            r = (e % 4) * CAP_C
                            ins = dve.scalar_tensor_tensor(out=ysc[r:r + CAP_C, s], in0=bank[CAP_X:S, :],
                                                           scalar=gate[CAP_X:S, e:e + 1], in1=g2[CAP_X:S, s],
                                                           op0=ALU.mult, op1=ALU.mult)
                        ins.then_inc(out_taken.sem, out_taken.one())

                def additions(q):
                    for i, (kind, j, t, h) in enumerate(order[q]):
                        n = before[q] + i
                        s = slice(h * HALF, h * HALF + HALF)
                        dst = X[:, t if kind == "x" else NT + t, s]
                        dve.wait_ge(add_filled.sem, n + 1)
                        dve.tensor_tensor(dst, dst, core.bank[5 + n % 3][:, :], ALU.add).then_inc(add_done.sem, add_done.one())
                    dve.wait_ge(add_done.sem, before[q + 1])

                for e in range(NE):
                    hidden(e)
                    if e % 2 == 0 and e:
                        additions(e // 2 - 1)
                    output(e)
                additions(NE // 2 - 1)


def feed_forward(core, I, C, X, layer, nx, mod_dram, sel_dram):
    with core.scope() as sb:
        xs = sb("expert_tokensT", [P, KT, NE, CAP_X + (CAP_C if nx > NT else 0)])
        with core.scope() as sb2:
            cols = sb2("mod_columns", [P, 2, 6, KT])
            modulation_columns(core, C, mod_dram, layer, cols[:, :, :, :].rearrange("p w j k -> p (w j k)"))
            route(core, I, C, X, layer, nx, cols, sel_dram, xs)
        experts(core, I, C, X, layer, nx, mod_dram, sel_dram, xs)



def conformer(core, I, C, hT, outT):
    nc = core.nc
    dve, act = nc.vector, nc.scalar
    step, landed, stored = core.step, core.landed, core.stored
    CT = CONV_CH // P
    PAD = (CONV_K - 1) // 2
    AT_C = SEQ + 2 * PAD
    WIDE = AT_C + CTX + 2 * PAD
    OUT = AT_C + CTX
    SPANS = ((0, 0, SEQ), (AT_C, SEQ, CTX))
    with core.scope() as sb:
        conv = sb("convolved", [P, CT, OUT])
        taps = sb("taps", [P, CT, CONV_K])
        cols = sb("ln_and_bias", [P, 3, CT])
        for j, name in enumerate(("cv_dw_b_2", "cv_ln_g_2", "cv_ln_b_2")):
            load_columns(core, cols[:, j, :], I[name], 0, CT)
        with core.scope() as sb2:
            rows = sb2("tap_rows", [CONV_K, CONV_CH])
            core.load(rows[:, :], I["cv_dw_w_2"][0])
            transposes(core, [(taps[:, :, :].rearrange("p c k -> p (c k)"),
                               [rows[:, c * P:c * P + P] for c in range(CT)])], C["ident"])
            h = sb2("padded", [P, CT, WIDE])
            gate = sb2("gate", [P, CT, ALLTOK])
            dve.wait_ge(step.sem, step.n)
            dve.memset(h[:, :, :], 0.0).then_inc(step.sem, step.one())

            def take(e, ct, t0, n, ps):
                if ct < CT:
                    at = PAD + (0 if t0 == 0 else AT_C)
                    return copy(core, e, h[:, ct, at:at + n], ps)
                return e.activation(gate[:, ct - CT, t0:t0 + n], ps, ACT.Sigmoid)

            half = CT * 2
            dense(core, hT, KT, ALLTOK, I["ev_w_in_2"][0], MLA_IN, 2 * CONV_CH, take, transposed=True,
                  who=lambda i: "v" if i < half else "s")
            for a, b, n in SPANS:
                s = h[:, :, a + PAD:a + PAD + n]
                dve.wait_ge(step.sem, step.n)
                dve.tensor_tensor(s, s, gate[:, :, b:b + n], ALU.mult).then_inc(step.sem, step.one())
            dve.wait_ge(step.sem, step.n)
            dve.wait_ge(landed.sem, landed.n)
            dve.wait_ge(stored.sem, stored.n)
            for k in range(CONV_K):
                for c in range(CT):
                    if k == 0:
                        ins = dve.tensor_scalar(conv[:, c, :], h[:, c, 0:OUT], taps[:, c, 0:1],
                                                cols[:, 0, c:c + 1], ALU.mult, ALU.add)
                    else:
                        ins = dve.scalar_tensor_tensor(out=conv[:, c, :], in0=h[:, c, k:k + OUT],
                                                       scalar=taps[:, c, k:k + 1], in1=conv[:, c, :],
                                                       op0=ALU.mult, op1=ALU.add)
                    ins.then_inc(core.link_v.sem, core.link_v.one())
                dve.wait_ge(core.link_v.sem, core.link_v.n)
            dve.tensor_copy(taps[:, 0, 0:1], taps[:, 0, 0:1]).then_inc(step.sem, step.one())
        with core.scope() as sb2:
            sq = sb2("squares", [P, CT, OUT])
            stat = sb2("statistic", [P, OUT])
            dve.wait_ge(step.sem, step.n)
            dve.memset(stat[:, :], 0.0).then_inc(step.sem, step.one())

            def total(src):
                def fill(pe, i, bank):
                    a, _, n = SPANS[i]
                    for c in range(CT):
                        ins = pe.matmul(bank[:, :n], C["ones"][:, 0, :], src[:, c, a:a + n],
                                        start=c == 0, stop=c == CT - 1)
                    return ins

                products(core, 2, fill, lambda e, i, bank: e.tensor_scalar(
                    stat[:, SPANS[i][0]:SPANS[i][0] + SPANS[i][2]], bank[:, :SPANS[i][2]],
                    1.0 / CONV_CH, None, ALU.mult))

            total(conv)
            dve.wait_ge(step.sem, step.n)
            dve.tensor_tensor(conv[:, :, :], conv[:, :, :], mid(stat[:, :], CT), ALU.subtract).then_inc(step.sem, step.one())
            act.wait_ge(step.sem, step.n)
            act.activation(sq[:, :, :], conv[:, :, :], ACT.Square).then_inc(step.sem, step.one())
            total(sq)
            rstd_of(core, stat[:, :], 1, EPS)
            dve.wait_ge(step.sem, step.n)
            dve.tensor_tensor(conv[:, :, :], conv[:, :, :], mid(stat[:, :], CT), ALU.mult).then_inc(step.sem, step.one())
            for c in range(CT):
                for a, b, n in SPANS:
                    act.wait_ge(step.sem, step.n)
                    act.activation(outT[:, c, b:b + n], conv[:, c, a:a + n], ACT.Silu,
                                    scale=cols[:, 1, c:c + 1], bias=cols[:, 2, c:c + 1]).then_inc(step.sem, step.one())


def rope(core, sb, x, tables):
    dve = core.nc.vector
    step, landed, stored = core.step, core.landed, core.stored
    half, q = ROPE // 2, ROPE // 4
    turned = sb("turned", [P, MH, ROPE])
    for t in range(NT):
        for j in range(2):
            for a in range(2):
                lo, other = j * half + a * q, j * half + (1 - a) * q
                dve.wait_ge(step.sem, step.n)
                dve.wait_ge(landed.sem, landed.n)
                dve.wait_ge(stored.sem, stored.n)
                dve.tensor_tensor(turned[:, :, lo:lo + q], x[:, t, :, other:other + q],
                                   mid(tables[:, 1, t, lo:lo + q], MH), ALU.mult).then_inc(step.sem, step.one())
        xt = x[:, t, :, :]
        dve.wait_ge(step.sem, step.n)
        dve.tensor_tensor(xt, xt, mid(tables[:, 0, t, :], MH), ALU.mult).then_inc(step.sem, step.one())
        dve.wait_ge(step.sem, step.n)
        dve.tensor_tensor(xt, xt, turned[:, :, :], ALU.add).then_inc(step.sem, step.one())


def latent_attention(core, I, C, um, outT):
    nc = core.nc
    dve, act = nc.vector, nc.scalar
    step, landed, stored = core.step, core.landed, core.stored
    KQ, KK = QL // P, KVL // P
    with core.scope() as sb:
        kv = sb("kv", [P, NX, MH, NOPE + MV])
        qT = sb("qT", [MQK, MH, ALLTOK])
        kTt = sb("kT", [MQK, MH, ALLTOK])
        with core.scope() as sb2:
            gains = sb2("latent_gains", [P, QL + KVL])
            head_gains = sb2("head_gains", [P, 2, MQK])
            tables = sb2("rope", [P, 2, NT, ROPE])
            load_rows(core, gains[:, 0:QL], I["mla_q_norm_2"], 0, QL)
            load_rows(core, gains[:, QL:], I["mla_kv_norm_2"], 0, KVL)
            load_rows(core, head_gains[:, 0, :], I["mla_q_g_2"], 0, MQK)
            load_rows(core, head_gains[:, 1, :], I["mla_k_g_2"], 0, MQK)
            for j in range(2):
                core.load(tables[:, j, :, :], I["rope"][j].rearrange("(t p) r -> p t r", p=P))
            with core.scope() as sb3:
                ckvT = sb3("ckvT", [P, KK, ALLTOK])
                x = um[:, :, QL:QL + KVL]
                rms_heads(core, x, NX, KVL, gains[:, QL:])
                transpose_tokens(core, x, ckvT, NX, C["ident"])
                dense(core, ckvT, KK, ALLTOK, I["mla_w_ukv_2"][0], 0, MH * (NOPE + MV),
                      lambda e, tt, col, n, ps: copy(
                          core, e, kv[:, tt, :, :].rearrange("p h n -> p (h n)")[:, col:col + n], ps))
            with core.scope() as sb3:
                full = sb3("q_or_k", [P, NX, MH, MQK])
                flat = full[:, :, :, :].rearrange("p t h n -> p (t h) n")
                for is_k in range(2):
                    if is_k:
                        dve.wait_ge(step.sem, step.n)
                        dve.tensor_copy(full[:, :, :, 0:NOPE], kv[:, :, :, 0:NOPE]).then_inc(step.sem, step.one())
                        for t in range(NX):
                            dve.wait_ge(step.sem, step.n)
                            dve.tensor_copy(full[:, t, :, NOPE:], mid(um[:, t, QL + KVL:], MH)).then_inc(step.sem, step.one())
                    else:
                        with core.scope() as sb4:
                            cqT = sb4("cqT", [P, KQ, ALLTOK])
                            x = um[:, :, 0:QL]
                            rms_heads(core, x, NX, QL, gains[:, 0:QL])
                            transpose_tokens(core, x, cqT, NX, C["ident"])
                            dense(core, cqT, KQ, ALLTOK, I["mla_w_uq_2"][0], 0, MH * MQK,
                                  lambda e, tt, col, n, ps: copy(
                                      core, e, full[:, tt, :, :].rearrange("p h n -> p (h n)")[:, col:col + n], ps))
                    rms_heads(core, flat, NX * MH, MQK, head_gains[:, is_k, :], 1.0 if is_k else MQK ** -0.5)
                    with core.scope() as sb4:
                        rope(core, sb4, full[:, 0:NT, :, NOPE:], tables)
                    dst = kTt if is_k else qT
                    jobs = []
                    for h in range(MH):
                        for a, b in ((0, NT), (NT, NX)):
                            jobs.append((dst[:, h, a * P:b * P], [full[:, t, h, :] for t in range(a, b)]))
                    transposes(core, jobs, C["ident"])
        with core.scope() as sb2:
            o = sb2("attended", [P, NX, MH * MV])
            s = sb2("scores", [P, NX, ALLTOK])
            pT = sb2("weightsT", [P, NX, ALLTOK])
            neg_max = sb2("neg_max", [P, NX])
            den = sb2("den", [P, NX])
            groups = [(t, a, n) for t in range(NT) for a, n in ((0, SEQ), (SEQ, CTX))]
            groups += [(t, SEQ, CTX) for t in range(NT, NX)]
            for h in range(MH):
                def fill(pe, i, bank):
                    t, a, n = groups[i]
                    return pe.matmul(bank[:, :n], qT[:, h, t * P:t * P + P], kTt[:, h, a:a + n], start=True, stop=True)

                def take(e, i, bank):
                    t, a, n = groups[i]
                    return copy(core, e, s[:, t, a:a + n], bank[:, :n])

                products(core, len(groups), fill, take, turns)
                softmax_rows(core, s[:, 0:NT, :], NT, ALLTOK, neg_max[:, 0:NT], den[:, 0:NT])
                softmax_rows(core, s[:, NT:NX, SEQ:], NC, CTX, neg_max[:, NT:], den[:, NT:])
                jobs = [(pT[:, kk, 0:SEQ], [s[:, t, kk * P:kk * P + P] for t in range(NT)]) for kk in range(NX)]
                jobs += [(pT[:, kk, SEQ:], [s[:, t, kk * P:kk * P + P] for t in range(NT, NX)]) for kk in range(NT, NX)]
                transposes(core, jobs, C["ident"])

                def fill(pe, t, bank):
                    first = 0 if t < NT else NT
                    for kk in range(first, NX):
                        ins = pe.matmul(bank[:, :MV], pT[:, kk, t * P:t * P + P], kv[:, kk, h, NOPE:],
                                        start=kk == first, stop=kk == NX - 1)
                    return ins

                products(core, NX, fill, lambda e, t, bank: e.tensor_scalar(
                    o[:, t, h * MV:(h + 1) * MV], bank[:, :MV], den[:, t:t + 1], None, ALU.mult))
            transpose_tokens(core, o, outT, NX, C["ident"])


def even_layer(core, I, C, X, mod_dram):
    nc = core.nc
    with core.scope() as sb:
        catT = sb("mixedT", [P, KT, ALLTOK])
        um = sb("latent_input", [P, NX, MLA_IN])
        with core.scope() as sb2:
            hT = sb2("hT", [P, KT, ALLTOK])
            with core.scope() as sb3:
                cols = sb3("mod_columns", [P, 2, 6, KT])
                scale = sb3("scale", [P, 2, KT])
                xn = sb3("normed", [P, NX, D])
                modulation_columns(core, C, mod_dram, 0, cols[:, :, :, :].rearrange("p w j k -> p (w j k)"))
                norm_scales(core, cols, I["norm1_g_2"], 0, SC1, scale[:, :, :])
                rms_tokens(core, sb3, X, xn, NX, D)
                modulated(core, xn, hT, scale, cols, SH1, C["ident"])
            dense(core, hT, KT, ALLTOK, I["ev_w_in_2"][0], 0, MLA_IN,
                  lambda e, tt, col, n, ps: copy(core, e, um[:, tt, col:col + n], ps))
            conformer(core, I, C, hT, catT[:, 4:8, :])
        latent_attention(core, I, C, um, catT[:, 0:4, :])
        gated_output(core, catT, I["ev_w_out_2"][0], X, mod_dram, 0, ALLTOK)



RCT = RD // P
LT_W, LT_A, LT_G = 3 * RCT, 3 * RCT + 1, 3 * RCT + 2
U_TILES = RW_IN // P
CTX_AT = SEQ + 2
U_WIDE = CTX_AT + CTX
RHO = float(np.exp(-0.5))
CH = 32
NCH = P // CH


def at_tile(t):
    return t * P if t < NT else CTX_AT + (t - NT) * P


def rwkv_inputs(core, I, C, hT, U):
    nc = core.nc
    dve, act = nc.vector, nc.scalar
    step, landed, stored = core.step, core.landed, core.stored
    with core.scope() as sb:
        wide = sb("padded", [P, U_TILES, U_WIDE + 2])
        taps = sb("taps", [P, U_TILES, SHIFT_K])
        rows = sb("tap_rows", [SHIFT_K, RW_IN])
        core.load(rows[:, :], I["rw_shift_w_2"][0])
        transposes(core, [(taps[:, :, :].rearrange("p c k -> p (c k)"),
                           [rows[:, c * P:c * P + P] for c in range(U_TILES)])], C["ident"])
        dve.wait_ge(step.sem, step.n)
        dve.memset(wide[:, :, :], 0.0).then_inc(step.sem, step.one())
        dense(core, hT, KT, ALLTOK, I["od_w_in_2"][0], 0, RW_IN,
              lambda e, ct, t0, n, ps: copy(
                  core, e, wide[:, ct, (1 if t0 == 0 else CTX_AT + 1):(1 if t0 == 0 else CTX_AT + 1) + n], ps),
              transposed=True, width=256)
        dve.wait_ge(step.sem, step.n)
        dve.wait_ge(landed.sem, landed.n)
        dve.wait_ge(stored.sem, stored.n)
        for k in range(SHIFT_K):
            for c in range(U_TILES):
                src = wide[:, c, k:k + U_WIDE]
                if k == 0:
                    ins = dve.tensor_scalar(U[:, c, :], src, taps[:, c, 0:1], None, ALU.mult)
                else:
                    ins = dve.scalar_tensor_tensor(out=U[:, c, :], in0=src, scalar=taps[:, c, k:k + 1],
                                                   in1=U[:, c, :], op0=ALU.mult, op1=ALU.add)
                ins.then_inc(core.link_v.sem, core.link_v.one())
            dve.wait_ge(core.link_v.sem, core.link_v.n)
        dve.tensor_copy(taps[:, 0, 0:1], taps[:, 0, 0:1]).then_inc(step.sem, step.one())
        act.wait_ge(step.sem, step.n)
        act.activation(U[:, LT_W, :], U[:, LT_W, :], ACT.Tanh).then_inc(step.sem, step.one())
        act.wait_ge(step.sem, step.n)
        act.activation(U[:, LT_G, :], U[:, LT_G, :], ACT.Sigmoid).then_inc(step.sem, step.one())


SHIFT_K = 3
COL_A0, COL_KK, COL_KA, COL_RK, COL_GG, COL_GB = 0, 2, 3, 4, 5, 6


def rows_of(R, d, at):
    return R[:, d * RH:(d + 1) * RH, at:at + RN].rearrange("p (e c) n -> p c e n", e=2)


def batched(core, jobs, start=True):
    def fill(pe, i, bank):
        dst, lhs, rhs, add = jobs[i // 4]
        for j in range(4):
            m = i % 4 * 4 + j
            ins = pe.matmul(bank[:, j * P:j * P + P], lhs[:, m, :], rhs[:, m, :], start=True, stop=True)
        return ins

    def take(e, i, bank):
        dst, lhs, rhs, add = jobs[i // 4]
        s = slice(i % 4 * 4, i % 4 * 4 + 4)
        src = bank[:, :].rearrange("p (m n) -> p m n", n=P)
        if add is None:
            return copy(core, e, dst[:, s, :], src)
        return e.tensor_tensor(dst[:, s, :], add[:, s, :], src, ALU.add)

    products(core, 4 * len(jobs), fill, take, lambda i: "s" if jobs[i // 4][3] is None else "v")


def place_of(d, h):
    return d * RH + h % 2 * (RH // 2) + h // 2


def grams(core, jobs):
    def fill(pe, i, bank):
        lhs, rhs, _ = jobs[i // 4]
        for j in range(4):
            d, e = i % 4 // 2, i % 2 * RN
            r = slice(e, e + RN)
            ins = pe.matmul(bank[:, j * P:j * P + P], lhs[r, d, j, :], rhs[r, d, j, :],
                            start=True, stop=True)
        return ins

    def take(e, i, bank):
        s = slice(i % 4 * 4, i % 4 * 4 + 4)
        d = i % 4 // 2
        for dst, mask in jobs[i // 4][2]:
            ins = e.tensor_tensor(dst[:, s, :], bank[:, :].rearrange("p (m n) -> p m n", n=P),
                                  mid(mask[d], 4), ALU.mult)
        return ins

    products(core, 4 * len(jobs), fill, take)


def rwkv(core, I, C, U, room, Y):
    nc = core.nc
    dve, act = nc.vector, nc.scalar
    step, landed, stored = core.step, core.landed, core.stored
    with core.scope() as sb:
        kkT = sb("kkT", [P, RCT, U_WIDE])
        vnat = sb("values", [P, NX, RD])
        w2 = sb("decay_up", [P, RD])
        a2 = sb("rate_up", [P, RD])
        w0 = sb("decay_base", [P, 2, RD])
        col = sb("columns", [P, 7, RCT])
        a0c = sb("rate_base", [P, 2, RCT])
        masks = sb("masks", [P, 2, 4, P])
        tri = sb("sums_in_chunk", [P, 2, 2, P])
        one_pair = sb("identity_and_zero", [P, 2, RCT, RN])
        core.load(w2[:, :], I["rw_w2_2"][0].rearrange("d r c -> (d r) c"))
        core.load(a2[:, :], I["rw_a2_2"][0].rearrange("d r c -> (d r) c"))
        for d in range(2):
            load_rows(core, w0[:, d, :], I["rw_w0_2"], d * RD, RD)
            load_columns(core, a0c[:, d, :], I["rw_a0_2"], d * RD, RCT)
            for kind in range(2):
                core.load(tri[:, d, kind, :], I["tri"][d, 2 * kind])
        core.load(masks[:, :, :, :], I["masks_f"].rearrange("d k s t -> s d k t"))
        for j, name in ((COL_KK, "rw_k_k_2"), (COL_KA, "rw_k_a_2"), (COL_RK, "rw_r_k_2"),
                        (COL_GG, "rw_gn_g_2"), (COL_GB, "rw_gn_b_2")):
            load_columns(core, col[:, j, :], I[name], 0, RCT)
        dve.wait_ge(step.sem, step.n)
        dve.wait_ge(landed.sem, landed.n)
        dve.wait_ge(stored.sem, stored.n)
        dve.memset(one_pair[:, :, :, :], 0.0).then_inc(step.sem, step.one())
        dve.wait_ge(step.sem, step.n)
        dve.tensor_tensor(one_pair[:, 0, :, :], mid(C["ident"][:, 0:RN], RCT),
                           mid(C["ident"][:, RN:P], RCT), ALU.add).then_inc(step.sem, step.one())
        for c in range(RCT):
            dve.wait_ge(step.sem, step.n)
            dve.tensor_scalar(kkT[:, c, :], U[:, RCT + c, :], col[:, COL_KK, c:c + 1], None, ALU.mult).then_inc(step.sem, step.one())
        with core.scope() as sb2:
            sq = sb2("squares", [P, RCT, U_WIDE])
            act.wait_ge(step.sem, step.n)
            act.activation(sq[:, :, :], kkT[:, :, :], ACT.Square).then_inc(step.sem, step.one())
            spans = [(c, a, n) for c in range(RCT) for a, n in ((0, SEQ), (SEQ, U_WIDE - SEQ))]

            def fill(pe, i, bank):
                c, a, n = spans[i]
                return pe.matmul(bank[:, :n], C["ones"][:, 1, :], sq[:, c, a:a + n], start=True, stop=True)

            def take(e, i, bank):
                c, a, n = spans[i]
                return e.tensor_scalar(sq[:, c, a:a + n], bank[:, :n], 1e-12, None, ALU.add)

            products(core, len(spans), fill, take)
            act.wait_ge(step.sem, step.n)
            act.activation(sq[:, :, :], sq[:, :, :], ACT.Sqrt).then_inc(step.sem, step.one())
            dve.wait_ge(step.sem, step.n)
            dve.reciprocal(sq[:, :, :], sq[:, :, :]).then_inc(step.sem, step.one())
            dve.wait_ge(step.sem, step.n)
            dve.tensor_tensor(kkT[:, :, :], kkT[:, :, :], sq[:, :, :], ALU.mult).then_inc(step.sem, step.one())
        transposes(core, [(vnat[:, t, :], [U[:, 2 * RCT + c, at_tile(t):at_tile(t) + P] for c in range(RCT)])
                          for t in range(NX)], C["ident"])
        dve.wait_ge(step.sem, step.n)
        dve.memset(Y, 0.0).then_inc(step.sem, step.one())
        with core.scope() as sb2:
            def matrices(n, view=None):
                return sb2(n, [P, 2 * RH, P])
            L = sb2("decay_or_bonus", [P, 2, RCT, P])
            Wc = sb2("decay_or_r", [P, 2, RCT, P])
            Wx = sb2("decay_before_or_a", [P, 2, RCT, P])
            Wi = sb2("inverse_decay_or_k", [P, 2, RCT, P])
            A = sb2("rate_or_b", [P, 2, RCT, P])
            kf = sb2("keys", [P, 2, RCT, P])
            bn = sb2("b_rows", [P, 2, RD])
            kn = sb2("k_rows", [P, 2, RD])
            S = sb2("states", [P, NCH + 1, 2, RCT, RN])
            edge = sb2("chunk_decay", [P, NCH, 2, RCT])
            B, Q, R = (room[:, 2 * i:2 * i + 2, :].rearrange("p a (m n) -> p (a m) n", n=P) for i in range(3))
            Lo, N2 = matrices("below_blocks"), matrices("n_or_squares")
            two = sb2("powers_then_steps", [P, 2, 2 * RH, P])
            Am, A2 = two[:, 0], two[:, 1]
            PH = two[:, :, :, :].rearrange("p a (i x) n -> p (a i) (x n)", i=2) \
                .rearrange("p i (d w y) -> p i d w y", d=2, w=2)
            dve.wait_ge(step.sem, step.n)
            dve.memset(S[:, 0], 0.0).then_inc(step.sem, step.one())
            orders = ([4, 5, 0, 1, 2, 3], [5, 4, 3, 2, 1, 0])
            for rnd in range(NX):
                tt = [orders[d][rnd] for d in range(2)]
                cs = [slice(at_tile(t), at_tile(t) + P) for t in tt]
                latent = rnd >= NC

                def fill(pe, i, bank):
                    d = i % 2
                    r = slice(d * LORA, d * LORA + LORA)
                    if i < 2:
                        return pe.matmul(bank[:, :], U[r, LT_W, cs[d]], w2[r, :], start=True, stop=True)
                    for c in range(RCT):
                        ins = pe.matmul(bank[:, c * P:c * P + P], a2[r, c * P:c * P + P], U[r, LT_A, cs[d]],
                                        start=True, stop=True)
                    return ins

                def take(e, i, bank):
                    d = i % 2
                    if i < 2:
                        return e.tensor_tensor(L[:, d, :, :].rearrange("p c n -> p (c n)"), bank[:, :], w0[:, d, :], ALU.add)
                    for c in range(RCT):
                        ins = e.activation(A[:, d, c, :], bank[:, c * P:c * P + P], ACT.Sigmoid,
                                           bias=a0c[:, d, c:c + 1])
                    return ins

                products(core, 4, fill, take, lambda i: "v" if i < 2 else "s")
                act.wait_ge(step.sem, step.n)
                act.activation(L[:, :, :, :], L[:, :, :, :], ACT.Sigmoid).then_inc(step.sem, step.one())

                def fill(pe, i, bank):
                    d, kind = i // 2, i % 2
                    for c in range(RCT):
                        ins = pe.matmul(bank[:, c * P:c * P + P], L[:, d, c, :], tri[:, d, kind, :],
                                        start=True, stop=True)
                    return ins

                def take(e, i, bank):
                    d, kind = i // 2, i % 2
                    src = bank[:, :].rearrange("p (c n) -> p c n", n=P)
                    if kind:
                        return e.activation(Wx[:, d], src, ACT.Exp, scale=-RHO)
                    e.activation(Wi[:, d], src, ACT.Exp, scale=RHO)
                    return e.activation(Wc[:, d], src, ACT.Exp, scale=-RHO)

                products(core, 4, fill, take, lambda i: "s")
                for i in range(NCH):
                    for d in range(2):
                        at = i * CH + CH - 1 if d == 0 else (NCH - 1 - i) * CH
                        dve.wait_ge(step.sem, step.n)
                        dve.tensor_copy(edge[:, i, d, :], Wc[:, d, :, at]).then_inc(step.sem, step.one())
                for d in range(2):
                    r_, k_ = U[:, 0:RCT, cs[d]], U[:, RCT:2 * RCT, cs[d]]
                    kk_ = kkT[:, :, cs[d]]
                    dve.wait_ge(step.sem, step.n)
                    dve.scalar_tensor_tensor(out=Wx[:, d], in0=kk_, scalar=-1.0, in1=Wx[:, d],
                                              op0=ALU.mult, op1=ALU.mult).then_inc(step.sem, step.one())
                    dve.wait_ge(step.sem, step.n)
                    dve.scalar_tensor_tensor(out=kf[:, d], in0=A[:, d], scalar=-1.0,
                                              in1=bc(col[:, COL_KA, :], P), op0=ALU.add, op1=ALU.mult).then_inc(step.sem, step.one())
                    dve.wait_ge(step.sem, step.n)
                    dve.scalar_tensor_tensor(out=kf[:, d], in0=kf[:, d], scalar=1.0, in1=k_,
                                              op0=ALU.add, op1=ALU.mult).then_inc(step.sem, step.one())
                    dve.wait_ge(step.sem, step.n)
                    dve.tensor_tensor(A[:, d], A[:, d], kk_, ALU.mult).then_inc(step.sem, step.one())
                    dve.wait_ge(step.sem, step.n)
                    dve.tensor_tensor(Wc[:, d], Wc[:, d], r_, ALU.mult).then_inc(step.sem, step.one())
                    dve.wait_ge(step.sem, step.n)
                    dve.tensor_tensor(L[:, d], kf[:, d], r_, ALU.mult).then_inc(step.sem, step.one())
                    dve.wait_ge(step.sem, step.n)
                    dve.tensor_tensor(L[:, d], L[:, d], bc(col[:, COL_RK, :], P), ALU.mult).then_inc(step.sem, step.one())
                dve.wait_ge(step.sem, step.n)
                dve.tensor_tensor(A[:, :, :, :], A[:, :, :, :], Wi[:, :, :, :], ALU.mult).then_inc(step.sem, step.one())
                dve.wait_ge(step.sem, step.n)
                dve.tensor_tensor(Wi[:, :, :, :], kf[:, :, :, :], Wi[:, :, :, :], ALU.mult).then_inc(step.sem, step.one())
                a_, b_, k2_, r2_ = Wx, A, Wi, Wc
                transposes(core, [(dst, [src[:, d, c, :] for c in range(RCT)]) for d in range(2)
                                  for dst, src in ((rows_of(R, d, 0), a_),
                                                   (bn[:, d, :], b_), (kn[:, d, :], k2_))], C["ident"])
                mk = lambda kind: [masks[:, d, kind, :] for d in range(2)]
                mk_t = lambda kind: [masks[:, 1 - d, kind, :] for d in range(2)]
                grams(core, [(b_, a_, [(B, mk(2)), (Lo, mk(3))]), (a_, b_, [(Am, mk_t(2))]),
                             (k2_, a_, [(N2, mk(1))])])

                def fill(pe, d, bank):
                    for h in range(RH):
                        ins = pe.matmul(bank[:, h * RN:h * RN + RN], N2[:, place_of(d, h), :],
                                        vnat[:, tt[d], h * RN:h * RN + RN], start=True, stop=True)
                    return ins

                products(core, 2, fill, lambda e, d, bank: e.tensor_copy(
                    rows_of(R, d, RN), bank[:, :].rearrange("p (c e n) -> p c e n", e=2, n=RN)))
                dve.wait_ge(step.sem, step.n)
                dve.tensor_tensor(Q, B, mid(C["ident"][:, :], 2 * RH), ALU.add).then_inc(step.sem, step.one())
                batched(core, [(N2, Am, B, None), (A2, B, Am, None)])
                batched(core, [(Q, A2, Q, Q), (B, A2, N2, None), (Am, N2, A2, None)])
                batched(core, [(Q, Am, Q, Q), (A2, B, Am, None)])
                batched(core, [(Q, A2, Q, Q)])
                batched(core, [(B, Q, R, None)])
                batched(core, [(R, Lo, B, R)])
                batched(core, [(B, Q, R, None)])
                if latent:
                    grams(core, [(b_, r2_, [(N2, mk(0))]), (k2_, r2_, [(Q, mk(0))])])

                def fill(pe, g, bank):
                    if g >= 2 * NCH:
                        d = g - 2 * NCH
                        for h in range(RH):
                            e = h % 2 * RN
                            ins = pe.matmul(bank[e:e + RN, h // 2 * P:h // 2 * P + P], B[:, place_of(d, h), 0:RN],
                                            N2[:, place_of(d, h), :], start=True, stop=True)
                        return ins
                    i, d = g // 2, g % 2
                    cc = i if d == 0 else NCH - 1 - i
                    r = slice(cc * CH, cc * CH + CH)
                    for h in range(RH):
                        e, m = h % 2 * RN, place_of(d, h)
                        n = slice(h * RN, h * RN + RN)
                        o = h // 2 * RN
                        pe.matmul(bank[e:e + RN, o:o + RN], B[r, m, 0:RN], bn[r, d, n], start=True, stop=True)
                        o += RCT * RN
                        pe.matmul(bank[e:e + RN, o:o + RN], bn[r, d, n], B[r, m, RN:], start=True, stop=False)
                        ins = pe.matmul(bank[e:e + RN, o:o + RN], kn[r, d, n], vnat[r, tt[d], n],
                                        start=False, stop=True)
                    return ins

                def take(e, g, bank):
                    if g >= 2 * NCH:
                        d = g - 2 * NCH
                        return e.tensor_tensor(r2_[:, d], r2_[:, d], bank[:, :].rearrange("p (c n) -> p c n", n=P),
                                               ALU.add)
                    i, d = g // 2, g % 2
                    return e.tensor_tensor(PH[:, i, d, :, :].rearrange("p w y -> p (w y)"), bank[:, :],
                                           one_pair[:, :, :, :].rearrange("p w c n -> p (w c n)"), ALU.add)

                products(core, 2 * NCH + (2 if latent else 0), fill, take)
                if rnd:
                    dve.wait_ge(step.sem, step.n)
                    dve.tensor_copy(S[:, 0], S[:, NCH]).then_inc(step.sem, step.one())
                v0 = core.emptied_v.n

                def fill(pe, i, bank):
                    pe.wait_ge(core.emptied_v.sem, v0 + i)
                    for d in range(2):
                        for h in range(RH):
                            e = h % 2 * RN
                            n = slice(h // 2 * RN, h // 2 * RN + RN)
                            o = d * RCT * RN + h // 2 * RN
                            ins = pe.matmul(bank[e:e + RN, o:o + RN], PH[e:e + RN, i, d, 0, n],
                                            S[e:e + RN, i, d, h // 2, :], start=True, stop=True)
                    return ins

                def take(e, i, bank):
                    new = S[:, i + 1].rearrange("p d c n -> p d (c n)")
                    linked(e, core.link_v, e.tensor_tensor(
                        new, bank[:, :].rearrange("p (d y) -> p d y", d=2), PH[:, i, :, 1, :], ALU.add))
                    flat = S[:, i + 1].rearrange("p d c n -> p (d c) n")
                    return e.tensor_tensor(flat, flat, bc(edge[:, i].rearrange("p d c -> p (d c)"), RN), ALU.mult)

                products(core, NCH, fill, take)
                if not latent:
                    continue

                def fill(pe, i, bank):
                    if i >= 2:
                        return pe.matmul(bank[:, :], C["ones"][:, 1, :],
                                         L[:, i - 2, :, :].rearrange("p c n -> p (c n)"), start=True, stop=True)
                    d = i
                    for h in range(RH):
                        e, m, o = h % 2 * RN, place_of(d, h), h // 2 * P
                        out = bank[e:e + RN, o:o + P]
                        pe.matmul(out, B[:, m, RN:], N2[:, m, :], start=h < 2, stop=False, skip_group_check=True)
                        pe.matmul(out, vnat[:, tt[d], h * RN:h * RN + RN], Q[:, m, :], start=False, stop=False,
                                  skip_group_check=True)
                        for n in range(NCH):
                            cc = n if d == 0 else NCH - 1 - n
                            ins = pe.matmul(bank[e:e + RN, o + cc * CH:o + cc * CH + CH],
                                            S[e:e + RN, n, d, h // 2, :], r2_[e:e + RN, d, h // 2, cc * CH:cc * CH + CH],
                                            start=False, stop=n == NCH - 1, skip_group_check=True)
                    return ins

                def take(e, i, bank):
                    d = i % 2
                    y = Y[:, :, tt[d] * P:tt[d] * P + P]
                    src = bank[:, :].rearrange("p (c n) -> p c n", n=P)
                    if i >= 2:
                        linked(e, core.link_v, e.tensor_tensor(L[:, d], src, U[:, 2 * RCT:3 * RCT, cs[d]], ALU.mult))
                        e.wait_ge(core.emptied_v.sem, core.emptied_v.n)
                        return e.tensor_tensor(y, y, L[:, d], ALU.add)
                    return e.tensor_tensor(y, y, src, ALU.add)

                products(core, 4, fill, take)
        with core.scope() as sb2:
            stat = sb2("statistic", [P, RCT, SEQ])
            sq = sb2("squares", [P, RCT, SEQ])
            g2 = sb2("gate_up", [P, RD])
            core.load(g2[:, :], I["rw_g2_2"][0])

            def total(src):
                products(core, RCT, lambda pe, i, bank: pe.matmul(bank[:, :], C["ones"][:, 1, :], src[:, i, :],
                                                                  start=True, stop=True),
                         lambda e, i, bank: e.tensor_scalar(stat[:, i, :], bank[:, :], 1.0 / RN, None, ALU.mult))

            total(Y)
            dve.wait_ge(step.sem, step.n)
            dve.tensor_tensor(Y, Y, stat[:, :, :], ALU.subtract).then_inc(step.sem, step.one())
            act.wait_ge(step.sem, step.n)
            act.activation(sq[:, :, :], Y, ACT.Square).then_inc(step.sem, step.one())
            total(sq)
            rstd_of(core, stat[:, :, :], 1, GN_EPS)
            dve.wait_ge(step.sem, step.n)
            dve.tensor_tensor(Y, Y, stat[:, :, :], ALU.mult).then_inc(step.sem, step.one())
            for c in range(RCT):
                dve.wait_ge(step.sem, step.n)
                dve.tensor_scalar(Y[:, c], Y[:, c], col[:, COL_GG, c:c + 1], col[:, COL_GB, c:c + 1],
                                   ALU.mult, ALU.add).then_inc(step.sem, step.one())
            products(core, RCT, lambda pe, i, bank: pe.matmul(bank[:, :], g2[:, i * P:i * P + P], U[:, LT_G, 0:SEQ],
                                                              start=True, stop=True),
                     lambda e, i, bank: e.tensor_tensor(Y[:, i, :], Y[:, i, :], bank[:, :], ALU.mult))


def neighbourhood(core, I, C, hT, outT):
    nc = core.nc
    dve, act = nc.vector, nc.scalar
    step, landed, stored = core.step, core.landed, core.stored
    W = NA_H * NA_D
    SPAN = 14
    with core.scope() as sb:
        v = sb("v", [P, NX, W])
        qT = sb("qT", [P, NA_H // 2, SEQ])
        kTt = sb("kT", [P, NA_H // 2, ALLTOK])
        gains = sb("gains", [P, 2, NA_D])
        load_rows(core, gains[:, 0, :], I["na_q_g_2"], 0, NA_D)
        load_rows(core, gains[:, 1, :], I["na_k_g_2"], 0, NA_D)
        for j, (dst, tokens) in enumerate(((qT, SEQ), (kTt, ALLTOK))):
            with core.scope() as sb2:
                x = sb2("q_or_k", [P, tokens // P, W])
                dense(core, hT, KT, tokens, I["od_w_in_2"][0], RW_IN + j * W, W,
                      lambda e, tt, col, n, ps: copy(core, e, x[:, tt, :], ps))
                rms_heads(core, x[:, :, :].rearrange("p t (h n) -> p (t h) n", n=NA_D), tokens // P * NA_H, NA_D,
                          gains[:, j, :], NA_D ** -0.5 if j == 0 else 1.0)
                transpose_tokens(core, x, dst, tokens // P, C["ident"])
        dense(core, hT, KT, ALLTOK, I["od_w_in_2"][0], RW_IN + 2 * W, W,
              lambda e, tt, col, n, ps: copy(core, e, v[:, tt, :], ps))
        o = sb("attended", [P, NT, W])
        s = sb("scores", [P, NT, ALLTOK])
        pT = sb("weightsT", [P, NX, SEQ])
        bias = sb("bias", [P, SPAN, GRID_W])
        window = sb("window", [P, GRID_W])
        neg_max = sb("neg_max", [P, NT])
        den = sb("den", [P, NT])
        core.load(window[:, :], I["window"])
        for h in range(NA_H):
            for r in range(2):
                core.load(bias[r * GRID_W:(r + 1) * GRID_W, :, :], I["rpb_windows"][h, :, 1 - r:1 - r + SPAN, :])
            dve.wait_ge(step.sem, step.n)
            dve.wait_ge(landed.sem, landed.n)
            dve.wait_ge(stored.sem, stored.n)
            dve.tensor_tensor(bias[:, :, :], bias[:, :, :], mid(window[:, :], SPAN), ALU.add).then_inc(step.sem, step.one())
            lo = h % 2 * NA_D

            def fill(pe, i, bank):
                t, c = i // 2, i % 2
                n = CTX if c else SEQ
                return pe.matmul(bank[:, :n], qT[lo:lo + NA_D, h // 2, t * P:t * P + P],
                                 kTt[lo:lo + NA_D, h // 2, c * SEQ:c * SEQ + n], start=True, stop=True)

            def take(e, i, bank):
                t, c = i // 2, i % 2
                if c:
                    return copy(core, e, s[:, t, SEQ:], bank[:, :CTX])
                return e.tensor_tensor(s[:, t, 0:SEQ], bank[:, :],
                                       bias[:, 6 - 2 * t:14 - 2 * t, :].rearrange("p x c -> p (x c)"), ALU.add)

            products(core, 2 * NT, fill, take, turns)
            softmax_rows(core, s[:, :, :], NT, ALLTOK, neg_max[:, :], den[:, :])
            transposes(core, [(pT[:, kk, :], [s[:, t, kk * P:kk * P + P] for t in range(NT)]) for kk in range(NX)],
                       C["ident"])

            def fill(pe, t, bank):
                for kk in range(NX):
                    ins = pe.matmul(bank[:, :NA_D], pT[:, kk, t * P:t * P + P], v[:, kk, h * NA_D:(h + 1) * NA_D],
                                    start=kk == 0, stop=kk == NX - 1)
                return ins

            products(core, NT, fill, lambda e, t, bank: e.tensor_scalar(
                o[:, t, h * NA_D:(h + 1) * NA_D], bank[:, :NA_D], den[:, t:t + 1], None, ALU.mult))
        transpose_tokens(core, o, outT, NT, C["ident"])


def odd_layer(core, I, C, X, mod_dram, spill):
    nc = core.nc

    def normed(hT):
        with core.scope() as sb3:
            cols = sb3("mod_columns", [P, 2, 6, KT])
            scale = sb3("scale", [P, 2, KT])
            xn = sb3("normed", [P, NX, D])
            modulation_columns(core, C, mod_dram, 1, cols[:, :, :, :].rearrange("p w j k -> p (w j k)"))
            norm_scales(core, cols, I["norm1_g_2"], 1, SC1, scale[:, :, :])
            rms_tokens(core, sb3, X, xn, NX, D)
            modulated(core, xn, hT, scale, cols, SH1, C["ident"])

    with core.scope() as sb:
        catT = sb("mixedT", [P, KT, SEQ])
        with core.scope() as sb2:
            U = sb2("inputsT", [P, U_TILES, U_WIDE])
            with core.scope() as sb3:
                hT = sb3("hT", [P, KT, ALLTOK])
                normed(hT)
                rwkv_inputs(core, I, C, hT, U)
            core.store(spill, X[:, :, :])
            rwkv(core, I, C, U, X, catT[:, 0:4, :])
            core.load(X[:, :, :], spill)
        with core.scope() as sb2:
            hT = sb2("hT", [P, KT, ALLTOK])
            normed(hT)
            neighbourhood(core, I, C, hT, catT[:, 4:8, :])
        gated_output(core, catT, I["od_w_out_2"][0], X, mod_dram, 1, SEQ)



def program(nc, I, out):
    core = Core(nc)
    mod_dram = nc.dram_tensor("modulation", (2, 2, MOD), F32).ap()
    sel_dram = nc.dram_tensor("selection", (4, NE * CAP_X), F32).ap()
    bias_dram = nc.dram_tensor("bias_of_distance", (NG, AH, REL_N), F32).ap()
    spill = nc.dram_tensor("rows_spilled", (P, NX, D), F32).ap()
    ident = nc.alloc_sbuf_tensor("identity", [P, P], F32)
    ones = nc.alloc_sbuf_tensor("ones", [P, 2, P], F32)
    X = nc.alloc_sbuf_tensor("rows", [P, NX, D], F32)
    C = {"ident": ident, "ones": ones}
    core.load(ident[:, :], I["ident"])
    core.load(ones[:, :, :], I["ones"].rearrange("d s t -> s d t"))
    core.load(X[:, 0:NT, :], I["x"][0].rearrange("(t p) d -> p t d", p=P))
    core.load(X[:, NT:NX, :], I["ctx_2"][0].rearrange("(t p) d -> p t d", p=P))
    copies = nc.dram_tensor("bias_copies", (NG, P, REL_N), F32).ap()
    first_block(core, I, C, X, bias_dram, copies)
    modulation(core, I, C, mod_dram)
    even_layer(core, I, C, X, mod_dram)
    feed_forward(core, I, C, X, 0, NX, mod_dram, sel_dram)
    odd_layer(core, I, C, X, mod_dram, spill)
    feed_forward(core, I, C, X, 1, NT, mod_dram, sel_dram)
    core.store(out[0].rearrange("(t p) d -> p t d", p=P), X[:, 0:NT, :])
    nc.sync.wait_ge(core.stored.sem, core.stored.n)


def rpb_windows(rpb):
    side = GRID_W - WIN_W
    padded = np.pad(np.asarray(rpb)[0], ((0, 0), (0, 0), (side, side)))
    return np.stack([padded[:, :, GRID_W - 1 - c:2 * GRID_W - 1 - c] for c in range(GRID_W)], axis=1)


def kernel(**inputs):
    import concourse.bacc as bacc
    from concourse.bass_utils import run_bass_kernel_spmd

    nc = bacc.Bacc("TRN2", target_bir_lowering=False, num_devices=1)
    arrays, I = {}, {}
    given = dict(inputs)
    given["rpb_windows"] = rpb_windows(given.pop("na_rpb_2"))
    given.update(shape_constants())
    for name, value in given.items():
        a = np.ascontiguousarray(value)
        arrays[f"in_{name}"] = a
        I[name] = nc.dram_tensor(f"in_{name}", a.shape, mybir.dt.from_np(a.dtype), kind="ExternalInput").ap()
    out = nc.dram_tensor("out", (1, SEQ, D), F32, kind="ExternalOutput").ap()
    program(nc, I, out)
    result = run_bass_kernel_spmd(nc, [arrays], core_ids=[0])
    return result.results[0]["out"]
```
